# Optimizing a Trainium2 kernel written in Bass

```python
import jax, jax.numpy as jnp
from jax import lax
import numpy as np
import math

D_MODEL = 1024
BATCH = 1
SEQ = 256
DEPTH = 1

N_MEM = 256
HEAD_DIM = 64
N_GMLP_GROUPS = 6
N_FOX_HEADS = 6
N_MEM_HEADS = 4
D_GMLP = N_GMLP_GROUPS * HEAD_DIM
D_FOX = N_FOX_HEADS * HEAD_DIM
D_MEMQ = N_MEM_HEADS * HEAD_DIM
D_MIX = D_GMLP + D_FOX + D_MEMQ
D_IN = 2 * D_GMLP + 3 * D_FOX + N_FOX_HEADS + D_MEMQ
CHUNK = 128
Q_BLOCK = 128
D_FF = 4 * D_MODEL
RMS_EPS = 1e-6
NEG_INF = -1e30


def rmsnorm(x, g):
    xf = x.astype(jnp.float32)
    y = xf * lax.rsqrt(jnp.mean(jnp.square(xf), axis=-1, keepdims=True) + RMS_EPS)
    return (y * g.astype(jnp.float32)).astype(x.dtype)

def gmlp_spatial_gating(u, v, w_s, b_s, v_norm_g):
    B, S, _ = u.shape
    n_chunks = S // CHUNK
    u = jax.nn.gelu(u)
    v = jax.nn.gelu(v).reshape(B, S, N_GMLP_GROUPS, HEAD_DIM)
    v = rmsnorm(v, v_norm_g.reshape(N_GMLP_GROUPS, HEAD_DIM))
    v = v.reshape(B, n_chunks, CHUNK, N_GMLP_GROUPS, HEAD_DIM)
    w_causal = jnp.tril(w_s)
    mixed = jnp.einsum('gts,bcsgd->bctgd', w_causal, v)
    mixed = mixed + b_s.T[None, None, :, :, None].astype(mixed.dtype)
    return u * mixed.reshape(B, S, D_GMLP)

def forgetting_attention(q, k, v, log_f):
    B, S, H, dh = q.shape
    scale = dh ** -0.5
    c = jnp.cumsum(log_f, axis=1).transpose(0, 2, 1)
    q = q.transpose(0, 2, 1, 3)
    k = k.transpose(0, 2, 1, 3)
    v = v.transpose(0, 2, 1, 3)
    outs = []
    for i in range(S // Q_BLOCK):
        start, end = i * Q_BLOCK, (i + 1) * Q_BLOCK
        qb = q[:, :, start:end]
        kb = k[:, :, :end]
        vb = v[:, :, :end]
        s = jnp.einsum('bhtd,bhsd->bhts', qb, kb).astype(jnp.float32) * scale
        s = s + c[:, :, start:end, None] - c[:, :, None, :end]
        mask = jnp.arange(end)[None, :] <= jnp.arange(start, end)[:, None]
        s = jnp.where(mask, s, NEG_INF)
        p = jax.nn.softmax(s, axis=-1).astype(vb.dtype)
        outs.append(jnp.einsum('bhts,bhsd->bthd', p, vb))
    o = jnp.concatenate(outs, axis=1)
    return o.reshape(B, S, H * dh)

def memory_cross_attention(qm, mem_n, w_kv):
    B, S, _ = qm.shape
    M = mem_n.shape[1]
    km, vm = jnp.split(mem_n @ w_kv, 2, axis=-1)
    q = qm.reshape(B, S, N_MEM_HEADS, HEAD_DIM)
    km = km.reshape(B, M, N_MEM_HEADS, HEAD_DIM)
    vm = vm.reshape(B, M, N_MEM_HEADS, HEAD_DIM)
    s = jnp.einsum('bthd,bmhd->bhtm', q, km).astype(jnp.float32) * (HEAD_DIM ** -0.5)
    p = jax.nn.softmax(s, axis=-1).astype(vm.dtype)
    o = jnp.einsum('bhtm,bmhd->bthd', p, vm)
    return o.reshape(B, S, D_MEMQ)

def first_inputs(seed: int = 0) -> dict:
    key = jax.random.key(seed)
    ks = jax.random.split(key, 17)
    f32 = jnp.float32

    def nrm(k, shape, scale):
        return jax.random.normal(k, shape, f32) * scale

    def gain(k, shape):
        return 1.0 + 0.05 * jax.random.normal(k, shape, f32)

    return {
        "x": jax.random.normal(ks[0], (BATCH, SEQ, D_MODEL), f32),
        "mem": jax.random.normal(ks[1], (BATCH, N_MEM, D_MODEL), f32),
        "norm_pre_mix": gain(ks[2], (DEPTH, D_MODEL)),
        "norm_post_mix": gain(ks[3], (DEPTH, D_MODEL)),
        "norm_pre_ffn": gain(ks[4], (DEPTH, D_MODEL)),
        "norm_post_ffn": gain(ks[5], (DEPTH, D_MODEL)),
        "norm_mem": gain(ks[6], (DEPTH, D_MODEL)),
        "w_in": nrm(ks[7], (DEPTH, D_MODEL, D_IN), D_MODEL ** -0.5),
        "b_forget": 3.0 + 0.5 * jax.random.normal(ks[8], (DEPTH, N_FOX_HEADS), f32),
        "gmlp_v_norm": gain(ks[9], (DEPTH, D_GMLP)),
        "gmlp_w_s": nrm(ks[10], (DEPTH, N_GMLP_GROUPS, CHUNK, CHUNK), CHUNK ** -0.5),
        "gmlp_b_s": 1.0 + 0.1 * jax.random.normal(ks[11], (DEPTH, N_GMLP_GROUPS, CHUNK), f32),
        "w_mem_kv": nrm(ks[12], (DEPTH, D_MODEL, 2 * D_MEMQ), D_MODEL ** -0.5),
        "w_out": nrm(ks[13], (DEPTH, D_MIX, D_MODEL), D_MIX ** -0.5),
        "w_ff1": nrm(ks[14], (DEPTH, D_MODEL, D_FF), D_MODEL ** -0.5),
        "w_ff2": nrm(ks[15], (DEPTH, D_FF, D_MODEL), D_FF ** -0.5),
    }

def first_block(x, mem, norm_pre_mix, norm_post_mix, norm_pre_ffn, norm_post_ffn, norm_mem,
              w_in, b_forget, gmlp_v_norm, gmlp_w_s, gmlp_b_s, w_mem_kv, w_out, w_ff1, w_ff2):
    splits = np.cumsum([D_GMLP, D_GMLP, D_FOX, D_FOX, D_FOX, N_FOX_HEADS]).tolist()
    B, S, _ = x.shape
    for l in range(DEPTH):
        h = rmsnorm(x, norm_pre_mix[l])
        z = h @ w_in[l]
        g_u, g_v, f_q, f_k, f_v, f_gate, m_q = jnp.split(z, splits, axis=-1)

        out_a = gmlp_spatial_gating(g_u, g_v, gmlp_w_s[l], gmlp_b_s[l], gmlp_v_norm[l])

        log_f = jax.nn.log_sigmoid((f_gate + b_forget[l]).astype(jnp.float32))
        out_b = forgetting_attention(
            f_q.reshape(B, S, N_FOX_HEADS, HEAD_DIM),
            f_k.reshape(B, S, N_FOX_HEADS, HEAD_DIM),
            f_v.reshape(B, S, N_FOX_HEADS, HEAD_DIM),
            log_f)

        mem_n = rmsnorm(mem, norm_mem[l])
        out_c = memory_cross_attention(m_q, mem_n, w_mem_kv[l])

        y = jnp.concatenate([out_a, out_b, out_c], axis=-1) @ w_out[l]
        x = x + rmsnorm(y, norm_post_mix[l])

        h = rmsnorm(x, norm_pre_ffn[l])
        f = jnp.square(jax.nn.relu(h @ w_ff1[l])) @ w_ff2[l]
        x = x + rmsnorm(f, norm_post_ffn[l])
    return x


DEPTH_2 = 2

N_MIXERS = 2
A_HEADS = 16
A_KV_HEADS = 2
A_HEAD_DIM = 64
WINDOW = 128
BLOCK = 128
NUM_BUCKETS = 32
MAX_DISTANCE = 128
B_HEADS = 16
Q_LORA = 256
KV_LORA = 128
QK_NOPE = 64
QK_ROPE = 32
V_DIM = 64
ROPE_BASE = 10000.0
D_FF_2 = 2816
EPS = 1e-6
NEG = -1e30

N_A_LAYERS = (DEPTH_2 + 1) // 2
N_B_LAYERS = DEPTH_2 // 2
A_IN_COLS = (A_HEADS + 2 * A_KV_HEADS) * A_HEAD_DIM
B_IN_COLS = Q_LORA + KV_LORA + QK_ROPE


def rmsnorm_2(x, g):
    xf = x.astype(jnp.float32)
    y = xf * lax.rsqrt(jnp.mean(xf * xf, axis=-1, keepdims=True) + EPS)
    return (y * g.astype(jnp.float32)).astype(x.dtype)

def swiglu(h, wg, wu, wd):
    return (jax.nn.silu(h @ wg) * (h @ wu)) @ wd

def t5_bucket(dist):
    n = jnp.maximum(dist, 0)
    max_exact = NUM_BUCKETS // 2
    large = max_exact + (jnp.log(jnp.maximum(n, 1).astype(jnp.float32) / max_exact)
                         / math.log(MAX_DISTANCE / max_exact)
                         * (NUM_BUCKETS - max_exact)).astype(jnp.int32)
    large = jnp.minimum(large, NUM_BUCKETS - 1)
    return jnp.where(n < max_exact, n, large)

def apply_rope(t, pos):
    half = QK_ROPE // 2
    inv_freq = ROPE_BASE ** (-jnp.arange(0, QK_ROPE, 2, dtype=jnp.float32) / QK_ROPE)
    ang = pos.astype(jnp.float32)[..., None] * inv_freq
    cos = jnp.cos(ang)[:, :, None, :]
    sin = jnp.sin(ang)[:, :, None, :]
    t1, t2 = t[..., :half].astype(jnp.float32), t[..., half:].astype(jnp.float32)
    return jnp.concatenate([t1 * cos - t2 * sin, t2 * cos + t1 * sin], axis=-1).astype(t.dtype)

def band(t, nb):
    B = t.shape[0]
    rest = t.shape[2:]
    pad = jnp.zeros((B, BLOCK) + rest, t.dtype)
    tp = jnp.concatenate([pad, t], axis=1).reshape((B, nb + 1, BLOCK) + rest)
    return jnp.concatenate([tp[:, :-1], tp[:, 1:]], axis=2)

def sliding_window_attention(h, pos, rel_bias, w_in, q_gain, k_gain, sinks, w_out):
    B, S, _ = h.shape
    nb = S // BLOCK
    G = A_HEADS // A_KV_HEADS
    qkv = h @ w_in
    q, k, v = jnp.split(qkv, [A_HEADS * A_HEAD_DIM, (A_HEADS + A_KV_HEADS) * A_HEAD_DIM], axis=-1)
    q = rmsnorm_2(q.reshape(B, S, A_HEADS, A_HEAD_DIM), q_gain)
    k = rmsnorm_2(k.reshape(B, S, A_KV_HEADS, A_HEAD_DIM), k_gain)
    v = v.reshape(B, S, A_KV_HEADS, A_HEAD_DIM)
    q = q.reshape(B, nb, BLOCK, A_KV_HEADS, G, A_HEAD_DIM)
    kb, vb = band(k, nb), band(v, nb)
    posb = band(pos, nb)
    scale = A_HEAD_DIM ** -0.5
    scores = jnp.einsum('bnqkgd,bnskd->bnkgqs', q, kb).astype(jnp.float32) * scale
    dist = pos.reshape(B, nb, BLOCK)[..., :, None] - posb[..., None, :]
    bias = rel_bias[t5_bucket(dist)].astype(jnp.float32)
    bias = bias.reshape(B, nb, BLOCK, 2 * BLOCK, A_KV_HEADS, G).transpose(0, 1, 4, 5, 2, 3)
    scores = scores + bias
    qi = jnp.arange(BLOCK)[:, None] + BLOCK
    si = jnp.arange(2 * BLOCK)[None, :]
    rel = qi - si
    blk = jnp.arange(nb)[:, None, None]
    valid = (rel >= 0) & (rel < WINDOW) & (blk * BLOCK + si - BLOCK >= 0)
    scores = jnp.where(valid[None, :, None, None], scores, NEG)
    sink = sinks.astype(jnp.float32).reshape(A_KV_HEADS, G)[None, None, :, :, None, None]
    m = jnp.maximum(jnp.max(scores, axis=-1, keepdims=True), sink)
    p = jnp.exp(scores - m)
    denom = jnp.sum(p, axis=-1, keepdims=True) + jnp.exp(sink - m)
    probs = (p / denom).astype(v.dtype)
    o = jnp.einsum('bnkgqs,bnskd->bnqkgd', probs, vb).reshape(B, S, A_HEADS * A_HEAD_DIM)
    return o @ w_out

def latent_attention(h, pos, w_in, q_norm, kv_norm, w_uq, w_ukv, q_gain, k_gain, w_out):
    B, S, _ = h.shape
    nb = S // BLOCK
    dqk = QK_NOPE + QK_ROPE
    c = h @ w_in
    c_q, c_kv, k_rope = jnp.split(c, [Q_LORA, Q_LORA + KV_LORA], axis=-1)
    q = (rmsnorm_2(c_q, q_norm) @ w_uq).reshape(B, S, B_HEADS, dqk)
    kv = (rmsnorm_2(c_kv, kv_norm) @ w_ukv).reshape(B, S, B_HEADS, QK_NOPE + V_DIM)
    k_nope, v = jnp.split(kv, [QK_NOPE], axis=-1)
    k = jnp.concatenate(
        [k_nope, jnp.broadcast_to(k_rope[:, :, None, :], (B, S, B_HEADS, QK_ROPE))], axis=-1)
    q = rmsnorm_2(q, q_gain)
    k = rmsnorm_2(k, k_gain)
    q = jnp.concatenate([q[..., :QK_NOPE], apply_rope(q[..., QK_NOPE:], pos)], axis=-1)
    k = jnp.concatenate([k[..., :QK_NOPE], apply_rope(k[..., QK_NOPE:], pos)], axis=-1)
    scale = dqk ** -0.5
    qb = q.reshape(B, nb, BLOCK, B_HEADS, dqk).transpose(1, 0, 2, 3, 4)
    key_idx = jnp.arange(S)

    def attend(args):
        q_blk, n = args
        s = jnp.einsum('bqhd,bshd->bhqs', q_blk, k).astype(jnp.float32) * scale
        q_idx = n * BLOCK + jnp.arange(BLOCK)
        s = jnp.where(key_idx[None, :] <= q_idx[:, None], s, NEG)
        p = jax.nn.softmax(s, axis=-1).astype(v.dtype)
        return jnp.einsum('bhqs,bshd->bqhd', p, v)

    o = lax.map(attend, (qb, jnp.arange(nb)))
    o = o.transpose(1, 0, 2, 3, 4).reshape(B, S, B_HEADS * V_DIM)
    return o @ w_out

def second_inputs(seed: int = 0) -> dict:
    key = jax.random.key(seed)
    ks = jax.random.split(key, 32)
    f32 = jnp.float32

    def w(k, shape, fan_in):
        return jax.random.normal(k, shape, f32) * (fan_in ** -0.5)

    def gain(k, shape):
        return 1.0 + 0.05 * jax.random.normal(k, shape, f32)

    x = jax.random.normal(ks[0], (BATCH, SEQ, D_MODEL), f32)
    offsets = jax.random.randint(ks[1], (BATCH, 1), 0, 64, dtype=jnp.int32)
    positions = (jnp.arange(SEQ, dtype=jnp.int32)[None, :] + offsets).astype(jnp.int32)
    return {
        "x": x,
        "positions": positions,
        "rel_bias": 0.5 * jax.random.normal(ks[2], (NUM_BUCKETS, A_HEADS), f32),
        "ffn_norm1": gain(ks[3], (DEPTH_2, D_MODEL)),
        "ffn1_wg": w(ks[4], (DEPTH_2, D_MODEL, D_FF_2), D_MODEL),
        "ffn1_wu": w(ks[5], (DEPTH_2, D_MODEL, D_FF_2), D_MODEL),
        "ffn1_wd": w(ks[6], (DEPTH_2, D_FF_2, D_MODEL), D_FF_2),
        "mix_norm": gain(ks[7], (DEPTH_2, D_MODEL)),
        "ffn_norm2": gain(ks[8], (DEPTH_2, D_MODEL)),
        "ffn2_wg": w(ks[9], (DEPTH_2, D_MODEL, D_FF_2), D_MODEL),
        "ffn2_wu": w(ks[10], (DEPTH_2, D_MODEL, D_FF_2), D_MODEL),
        "ffn2_wd": w(ks[11], (DEPTH_2, D_FF_2, D_MODEL), D_FF_2),
        "a_w_in": w(ks[12], (N_A_LAYERS, D_MODEL, A_IN_COLS), D_MODEL),
        "a_q_gain": gain(ks[13], (N_A_LAYERS, A_HEAD_DIM)),
        "a_k_gain": gain(ks[14], (N_A_LAYERS, A_HEAD_DIM)),
        "a_sinks": jax.random.normal(ks[15], (N_A_LAYERS, A_HEADS), f32),
        "a_w_out": w(ks[16], (N_A_LAYERS, A_HEADS * A_HEAD_DIM, D_MODEL), A_HEADS * A_HEAD_DIM),
        "b_w_in": w(ks[17], (N_B_LAYERS, D_MODEL, B_IN_COLS), D_MODEL),
        "b_q_norm": gain(ks[18], (N_B_LAYERS, Q_LORA)),
        "b_kv_norm": gain(ks[19], (N_B_LAYERS, KV_LORA)),
        "b_w_uq": w(ks[20], (N_B_LAYERS, Q_LORA, B_HEADS * (QK_NOPE + QK_ROPE)), Q_LORA),
        "b_w_ukv": w(ks[21], (N_B_LAYERS, KV_LORA, B_HEADS * (QK_NOPE + V_DIM)), KV_LORA),
        "b_q_gain": gain(ks[22], (N_B_LAYERS, QK_NOPE + QK_ROPE)),
        "b_k_gain": gain(ks[23], (N_B_LAYERS, QK_NOPE + QK_ROPE)),
        "b_w_out": w(ks[24], (N_B_LAYERS, B_HEADS * V_DIM, D_MODEL), B_HEADS * V_DIM),
    }

def second_block(x, positions, rel_bias, ffn_norm1, ffn1_wg, ffn1_wu, ffn1_wd, mix_norm,
              ffn_norm2, ffn2_wg, ffn2_wu, ffn2_wd, a_w_in, a_q_gain, a_k_gain, a_sinks,
              a_w_out, b_w_in, b_q_norm, b_kv_norm, b_w_uq, b_w_ukv, b_q_gain, b_k_gain,
              b_w_out):
    for i in range(DEPTH_2):
        x = x + 0.5 * swiglu(rmsnorm_2(x, ffn_norm1[i]), ffn1_wg[i], ffn1_wu[i], ffn1_wd[i])
        h = rmsnorm_2(x, mix_norm[i])
        j = i // N_MIXERS
        if i % N_MIXERS == 0:
            x = x + sliding_window_attention(h, positions, rel_bias, a_w_in[j], a_q_gain[j],
                                             a_k_gain[j], a_sinks[j], a_w_out[j])
        else:
            x = x + latent_attention(h, positions, b_w_in[j], b_q_norm[j], b_kv_norm[j],
                                     b_w_uq[j], b_w_ukv[j], b_q_gain[j], b_k_gain[j], b_w_out[j])
        x = x + 0.5 * swiglu(rmsnorm_2(x, ffn_norm2[i]), ffn2_wg[i], ffn2_wu[i], ffn2_wd[i])
    return x


def setup_inputs(seed=0):
    out = dict(first_inputs(seed))
    for name, value in second_inputs(seed + 1).items():
        if name != "x":
            out[name + "_2"] = value
    return out


def reference(
    x, mem, norm_pre_mix, norm_post_mix, norm_pre_ffn, norm_post_ffn, norm_mem, w_in, b_forget,
    gmlp_v_norm, gmlp_w_s, gmlp_b_s, w_mem_kv, w_out, w_ff1, w_ff2, positions_2, rel_bias_2,
    ffn_norm1_2, ffn1_wg_2, ffn1_wu_2, ffn1_wd_2, mix_norm_2, ffn_norm2_2, ffn2_wg_2, ffn2_wu_2,
    ffn2_wd_2, a_w_in_2, a_q_gain_2, a_k_gain_2, a_sinks_2, a_w_out_2, b_w_in_2, b_q_norm_2,
    b_kv_norm_2, b_w_uq_2, b_w_ukv_2, b_q_gain_2, b_k_gain_2, b_w_out_2,
):
    x = first_block(
        x, mem, norm_pre_mix, norm_post_mix, norm_pre_ffn, norm_post_ffn, norm_mem, w_in,
        b_forget, gmlp_v_norm, gmlp_w_s, gmlp_b_s, w_mem_kv, w_out, w_ff1, w_ff2,
    )
    return second_block(
        x, positions_2, rel_bias_2, ffn_norm1_2, ffn1_wg_2, ffn1_wu_2, ffn1_wd_2, mix_norm_2,
        ffn_norm2_2, ffn2_wg_2, ffn2_wu_2, ffn2_wd_2, a_w_in_2, a_q_gain_2, a_k_gain_2,
        a_sinks_2, a_w_out_2, b_w_in_2, b_q_norm_2, b_kv_norm_2, b_w_uq_2, b_w_ukv_2,
        b_q_gain_2, b_k_gain_2, b_w_out_2,
    )


_drawn_inputs = setup_inputs


def setup_inputs(seed=0):
    import zlib

    import numpy as np

    out = dict(_drawn_inputs(seed))
    spreads = {}
    factors = {'norm_mem': 8.0,
     'gmlp_v_norm': 3.056,
     'ffn_norm1_2': 3.314,
     'mix_norm_2': 3.024,
     'ffn_norm2_2': 3.421,
     'a_q_gain_2': 8.0,
     'a_k_gain_2': 8.0,
     'a_sinks_2': 4.31,
     'b_q_norm_2': 8.0,
     'b_kv_norm_2': 5.047,
     'b_q_gain_2': 8.0,
     'b_k_gain_2': 8.0}
    for name, (base, spread) in spreads.items():
        noise = np.random.default_rng([zlib.crc32(name.encode()), seed]).standard_normal(out[name].shape)
        drawn = base * np.exp(spread * noise) if base else spread * noise
        out[name] = __import__('jax').numpy.asarray(drawn.astype(out[name].dtype))
    for name, factor in factors.items():
        out[name] = (out[name] * factor).astype(out[name].dtype)
    return out
```

```python
import math
from contextlib import ExitStack

import concourse.bass as bass
from concourse import mybir

F32 = mybir.dt.float32
F32R = mybir.dt.float32r
I32 = mybir.dt.int32
ALU = mybir.AluOpType
ACT = mybir.ActivationFunctionType
AX = mybir.AxisListType

P = 128
TT = 2
TOK = TT * P
D = 1024
KD = D // P
HD = 64
EPS = 1e-6
NEG = -1e30

RAW = 6
RING = 3
BLK = 2048

STAGES = ["M1", "F0", "F1", "MA", "F2", "F3", "MB", "F4"]


def build(nc, i, out):
    blocks = []
    first = {}

    def columns(w, c, n):
        return w[:, c:c + n].rearrange("(k p) n -> p k n", p=P)

    FF0, FF = 4096, 2816
    I0, I1 = FF0 // 256, FF // 256
    first["kv"] = len(blocks)
    blocks += [columns(i["w_mem_kv"][0], c, 256) for c in (0, 256)]
    first["in"] = len(blocks)
    w_in_cuts = [(0, 256), (256, 256), (512, 256), (768, 256), (1024, 256), (1280, 256),
                 (1536, 256), (1792, 134), (1926, 256)]
    blocks += [columns(i["w_in"][0], c, n) for c, n in w_in_cuts]
    first["out"] = len(blocks)
    blocks += [columns(i["w_out"][0], c, 256) for c in range(0, D, 256)]
    first["F0"] = len(blocks)
    for s in range(I0 + 1 if "F0" in STAGES else 0):
        if s < I0:
            blocks.append(columns(i["w_ff1"][0], 256 * s, 256))
        if s:
            blocks.append(i["w_ff2"][0][256 * (s - 1):256 * s, :].rearrange("(k p) n -> p k n", p=P))
    swiglu = {"F1": ("ffn1", 0), "F2": ("ffn2", 0), "F3": ("ffn1", 1), "F4": ("ffn2", 1)}

    def swiglu_weights(stage):
        name, layer = swiglu[stage]
        return [i[f"{name}_w{x}_2"][layer] for x in "gud"]

    def swiglu_blocks(stage):
        wg, wu, wd = swiglu_weights(stage)
        first[stage] = len(blocks)
        for s in range(I1 + 1):
            if s < I1:
                blocks.append(columns(wg, 256 * s, 256))
                blocks.append(columns(wu, 256 * s, 256))
            if s:
                blocks.append(wd[256 * (s - 1):256 * s, :].rearrange("(k p) n -> p k n", p=P))

    if "F1" in STAGES:
        swiglu_blocks("F1")
    if "MA" in STAGES:
        first["a_in"] = len(blocks)
        blocks += [columns(i["a_w_in_2"][0], c, 256) for c in range(0, 1280, 256)]
        first["a_out"] = len(blocks)
        blocks += [columns(i["a_w_out_2"][0], c, 256) for c in range(0, D, 256)]
    if "F2" in STAGES:
        swiglu_blocks("F2")
        swiglu_blocks("F3")
    if "MB" in STAGES:
        first["b_in"] = len(blocks)
        blocks += [columns(i["b_w_in_2"][0], c, n) for c, n in ((0, 256), (256, 160))]
        first["b_up"] = len(blocks)
        blocks += [columns(i["b_w_uq_2"][0], c, n) for c, n in ((0, 1024), (1024, 512))]
        blocks += [columns(i["b_w_ukv_2"][0], 0, 2048)]
        first["b_out"] = len(blocks)
        blocks += [columns(i["b_w_out_2"][0], c, 256) for c in range(0, D, 256)]
    if "F4" in STAGES:
        swiglu_blocks("F4")
    NB = len(blocks)

    gains = [i["norm_mem"][0], i["norm_pre_mix"][0], i["norm_post_mix"][0], i["norm_pre_ffn"][0],
             i["norm_post_ffn"][0], i["ffn_norm1_2"][0], i["mix_norm_2"][0], i["ffn_norm2_2"][0],
             i["ffn_norm1_2"][1], i["mix_norm_2"][1], i["ffn_norm2_2"][1]]
    GS = 2

    with ExitStack() as ctx:
        def sb(name, shape, dt=F32):
            return ctx.enter_context(nc.sbuf_tensor(name, shape, dt))

        def sem(name):
            return ctx.enter_context(nc.semaphore(name))

        raw = sb("raw", [P, RAW, BLK])
        w_hi = sb("w_hi", [P, RING, BLK], F32R)
        w_lo = sb("w_lo", [P, RING, BLK], F32R)
        x = sb("x", [P, TT, D])
        h_hi = sb("h_hi", [P, KD, TOK], F32R)
        h_lo = sb("h_lo", [P, KD, TOK], F32R)
        scratch = sb("scratch", [P, 3 * D])
        xn = scratch[:, 0:2 * D].rearrange("p (t d) -> p t d", t=TT)
        junk = scratch[:, 2 * D:3 * D]
        act = sb("act", [P, 3, 512])
        act_hi = sb("act_hi", [P, 3, 512], F32R)
        act_lo = sb("act_lo", [P, 3, 512], F32R)
        gain = sb("gain", [P, GS, D])
        arena = sb("arena", [P, 10700])
        ident = sb("ident", [P, P])
        tri = sb("tri", [P, 3 * P])
        causal = sb("causal", [P, 3 * P])
        sums = sb("sums", [P, 64])
        rstd = sb("rstd", [P, 64])
        small = sb("small", [P, 256])
        keep = sb("keep", [P, 544])
        halves = sb("halves", [P, 36])
        ps = ctx.enter_context(nc.psum_tensor("ps", [P, 8, 512], F32))

        landed = [sem(f"landed{s}") for s in range(RAW)]
        hi_ready = sem("hi_ready")
        lo_ready = sem("lo_ready")
        block_used = sem("block_used")
        gain_landed = [sem(f"gain_landed{s}") for s in range(GS)]
        gain_used = sem("gain_used")
        mem_landed = sem("mem_landed")
        x_landed = sem("x_landed")
        tables_ready = sem("tables_ready")
        dve_step = sem("dve_step")
        act_step = sem("act_step")
        pool_step = sem("pool_step")
        sumsq_ready = sem("sumsq_ready")
        xn_ready = sem("xn_ready")
        h_psum = sem("h_psum")
        h_hi_ready = sem("h_hi_ready")
        h_lo_ready = sem("h_lo_ready")
        y_sumsq = sem("y_sumsq")
        norm_rstd = sem("norm_rstd")
        y_rstd = sem("y_rstd")
        v_sumsq = sem("v_sumsq")
        v_rstd = sem("v_rstd")
        x_ready = sem("x_ready")
        out_landed = sem("out_landed")

        chain = {"dve": 0, "act": 0, "pool": 0}

        def dve_then(instruction):
            chain["dve"] += 1
            instruction.then_inc(dve_step, 1)
            nc.vector.wait_ge(dve_step, chain["dve"])

        def act_then(instruction):
            chain["act"] += 1
            instruction.then_inc(act_step, 1)
            nc.scalar.wait_ge(act_step, chain["act"])

        def pool_then(instruction):
            chain["pool"] += 1
            instruction.then_inc(pool_step, 1)
            nc.gpsimd.wait_ge(pool_step, chain["pool"])

        def view(ring, slot, b_shape):
            k, n = b_shape
            return ring[:, slot, 0:k * n].rearrange("p (k n) -> p k n", k=k)

        def shape(b):
            return blocks[b].shape[1], blocks[b].shape[2]

        def parts(b):
            return view(w_hi, b % RING, shape(b)), view(w_lo, b % RING, shape(b))

        def load(b, source=None, turn=0):
            if b >= RAW:
                nc.sync.wait_ge(lo_ready, b - RAW + 1 + RAW * turn)
            source = blocks[b] if source is None else source
            nc.sync.dma_start(view(raw, b % RAW, shape(b)), source).then_inc(landed[b % RAW], 16)

        def size(b):
            k, n = shape(b)
            return k * n

        def round_block(b, turn=0):
            if b >= NB:
                return
            if b >= RING:
                nc.scalar.wait_ge(block_used, b - RING + 1 + RAW * turn)
            nc.scalar.wait_ge(landed[b % RAW], 16 * (b // RAW + 1) + 16 * turn)
            n = size(b)
            nc.scalar.copy(w_hi[:, b % RING, 0:n], raw[:, b % RAW, 0:n]).then_inc(hi_ready, 1)

        def split_block(b, turn=0):
            if b >= NB:
                return
            nc.vector.wait_ge(hi_ready, b + 1 + RAW * turn)
            n = size(b)
            nc.vector.tensor_tensor(w_lo[:, b % RING, 0:n], raw[:, b % RAW, 0:n],
                                    w_hi[:, b % RING, 0:n].bitcast(F32), ALU.subtract).then_inc(lo_ready, 1)

        def product(to, still, moving, start, stop):
            nc.tensor.matmul(to, still[0], moving[0], start=start, stop=False, skip_group_check=True)
            nc.tensor.matmul(to, still[0], moving[1], start=False, stop=False, skip_group_check=True)
            return nc.tensor.matmul(to, still[1], moving[0], start=False, stop=stop, skip_group_check=True)

        def features_out(b, to, kn=KD, turn=0, wait_h=None):
            nc.tensor.wait_ge(lo_ready, b + 1 + RAW * turn)
            hi, lo = parts(b)
            k_n, cols = shape(b)
            for f in range(cols // P):
                for k in range(k_n):
                    if wait_h is not None and f == 0 and k % 2 == 0:
                        nc.tensor.wait_ge(h_lo_ready, wait_h + k // 2 + 1)
                    last = product(to(f), (hi[:, k, f * P:(f + 1) * P], lo[:, k, f * P:(f + 1) * P]),
                                   (h_hi[:, k, :], h_lo[:, k, :]), k == 0, k == k_n - 1)
            last.then_inc(block_used, 1)

        def tokens_out(b, to, turn=0, wait_h=None, h0=0):
            nc.tensor.wait_ge(lo_ready, b + 1 + RAW * turn)
            hi, lo = parts(b)
            k_n, cols = shape(b)
            for t in range(TT):
                for c in range(0, cols, 512):
                    w = min(512, cols - c)
                    for k in range(k_n):
                        if wait_h is not None and t == 0 and c == 0 and k % 2 == 0:
                            nc.tensor.wait_ge(h_lo_ready, wait_h + k // 2 + 1)
                        last = product(to(t, c, w), (h_hi[:, h0 + k, t * P:(t + 1) * P], h_lo[:, h0 + k, t * P:(t + 1) * P]),
                                       (hi[:, k, c:c + w], lo[:, k, c:c + w]), k == 0, k == k_n - 1)
            last.then_inc(block_used, 1)

        def y_bank(t, c, w):
            return ps[:, 4 + 2 * t + c // 512, c % 512:c % 512 + w]

        squares = {"h": 0, "y": 0}

        def junk_free():
            if squares["h"]:
                nc.scalar.wait_ge(sumsq_ready, squares["h"])
            if squares["y"]:
                nc.scalar.wait_ge(y_sumsq, squares["y"])

        def norm_scalar_sums(n, source, ready):
            for t in range(TT):
                ready(nc.scalar, t)
                junk_free()
                squares["h"] += 1
                nc.scalar.activation(junk, source[:, t, :], ACT.Square,
                                     accum_out=sums[:, 2 * n + t:2 * n + t + 1]).then_inc(sumsq_ready, 1)

        def rsqrt_pool(to, sums_of, count, done, eps=EPS):
            n = sums_of.shape[1]
            pool_then(nc.gpsimd.tensor_scalar(to, sums_of, 1.0 / count, eps, ALU.mult, ALU.add))
            nc.gpsimd.tensor_tensor(to, to, halves[:, 0:n], ALU.pow).then_inc(done, 1)

        def norm_pool(n):
            for t in range(TT):
                c = 2 * n + t
                nc.gpsimd.wait_ge(sumsq_ready, c + 1)
                rsqrt_pool(rstd[:, c:c + 1], sums[:, c:c + 1], D, norm_rstd)

        def add_normed_pool(m):
            for t in range(TT):
                c = 32 + 2 * m + t
                nc.gpsimd.wait_ge(y_sumsq, 2 * m + t + 1)
                rsqrt_pool(rstd[:, c:c + 1], sums[:, c:c + 1], D, y_rstd)

        def gain_wait(g):
            nc.vector.wait_ge(gain_landed[g % GS], 16 * (g // GS + 1))

        def norm_vector_scale(n, g, source):
            for t in range(TT):
                c = 2 * n + t
                nc.vector.wait_ge(norm_rstd, c + 1)
                if t == 0:
                    gain_wait(g)
                    if n:
                        nc.vector.wait_ge(h_psum, 4 * n)
                last = nc.vector.scalar_tensor_tensor(xn[:, t, :], source[:, t, :], rstd[:, c:c + 1],
                                                      gain[:, g % GS, :], ALU.mult, ALU.mult)
                last.then_inc(xn_ready, 1)

        def norm_tensor_turn(n):
            for t in range(TT):
                nc.tensor.wait_ge(xn_ready, 2 * n + t + 1)
                for k in range(KD):
                    col = (k % 2) * TOK + t * P
                    last = nc.tensor.transpose(ps[:, k // 2, col:col + P], xn[:, t, k * P:(k + 1) * P], ident[:, :])
                    if t == TT - 1 and k % 2:
                        last.then_inc(h_psum, 1)

        def norm_scalar_round(n):
            for j in range(4):
                nc.scalar.wait_ge(h_psum, 4 * n + j + 1)
                nc.scalar.copy(h_hi[:, 2 * j:2 * j + 2, :], ps[:, j, :].rearrange("p (k t) -> p k t", k=2)).then_inc(h_hi_ready, 1)

        def norm_vector_split(n):
            for j in range(4):
                nc.vector.wait_ge(h_hi_ready, 4 * n + j + 1)
                nc.vector.tensor_tensor(h_lo[:, 2 * j:2 * j + 2, :], ps[:, j, :].rearrange("p (k t) -> p k t", k=2),
                                        h_hi[:, 2 * j:2 * j + 2, :].bitcast(F32), ALU.subtract).then_inc(h_lo_ready, 1)

        def y_block(r):
            return [first["out"] + 3, first["F0"] + 2 * I0 - 1,
                    first.get("F1", 0) + 3 * I1 - 1, first.get("a_out", 0) + 3, first.get("F2", 0) + 3 * I1 - 1,
                    first.get("F3", 0) + 3 * I1 - 1, first.get("b_out", 0) + 3, first.get("F4", 0) + 3 * I1 - 1][r]

        def add_scaled(r, scale):
            nc.vector.wait_ge(block_used, y_block(r) + 1)
            for t in range(TT):
                nc.vector.scalar_tensor_tensor(x[:, t, :], ps[:, 4 + 2 * t:6 + 2 * t, :].rearrange("p b c -> p (b c)"), scale,
                                               x[:, t, :], ALU.mult, ALU.add).then_inc(x_ready, 1)

        def add_normed_scalar(r, m):
            nc.scalar.wait_ge(block_used, y_block(r) + 1)
            for t in range(TT):
                junk_free()
                squares["y"] += 1
                nc.scalar.activation(junk, ps[:, 4 + 2 * t:6 + 2 * t, :].rearrange("p b c -> p (b c)"), ACT.Square,
                                     accum_out=sums[:, 32 + 2 * m + t:33 + 2 * m + t]).then_inc(y_sumsq, 1)

        def add_normed_vector(r, m, g):
            for t in range(TT):
                c = 32 + 2 * m + t
                nc.vector.wait_ge(y_rstd, 2 * m + t + 1)
                if t == 0:
                    gain_wait(g)
                    nc.vector.wait_ge(h_psum, 4 * (2 + m))
                dve_then(nc.vector.scalar_tensor_tensor(xn[:, t, :], ps[:, 4 + 2 * t:6 + 2 * t, :].rearrange("p b c -> p (b c)"),
                                                        rstd[:, c:c + 1], gain[:, g % GS, :], ALU.mult, ALU.mult))
                last = nc.vector.tensor_tensor(x[:, t, :], x[:, t, :], xn[:, t, :], ALU.add)
                last.then_inc(x_ready, 1)

        def x_after(r):
            def wait(engine, t):
                engine.wait_ge(x_ready, 2 * r + t + 1)
            return wait

        def carve(at, *dims):
            n = 1
            for d in dims:
                n *= d
            ap = arena[:, at:at + n]
            if len(dims) == 2:
                ap = ap.rearrange("p (a b) -> p a b", a=dims[0])
            elif len(dims) == 3:
                ap = ap.rearrange("p (a b c) -> p a b c", a=dims[0], b=dims[1])
            return ap

        S_AT = 10700 - 2 * 1024
        prob = carve(S_AT, 2, 512)
        prob_t = carve(S_AT + 1024, 2, 512)
        mx, nmx, den, rden, sink_e = (small[:, 160 + 4 * n:164 + 4 * n].rearrange("p (b t) -> p b t", b=2) for n in range(5))
        scores_psum = sem("scores_psum")
        negmax_ready = sem("negmax_ready")
        exp_ready = sem("exp_ready")
        prob_ready = sem("prob_ready")
        turned_psum = sem("turned_psum")
        turned_ready = sem("turned_ready")
        o_psum = sem("o_psum")
        o_hi_ready = sem("o_hi_ready")
        o_lo_ready = sem("o_lo_ready")

        class Head:

            def __init__(self, e, q, k, v, mask, scale, tile, row, causal=True, extra=None, sink=None,
                         wait_tensor=None, wait_vector=None):
                self.e, self.q, self.k, self.v, self.mask, self.scale = e, q, k, v, mask, scale
                self.tile, self.row, self.causal, self.extra, self.sink = tile, row, causal, extra, sink
                self.wait_tensor, self.wait_vector = wait_tensor, wait_vector

            def keys(self, t):
                return (t + 1) * P if self.causal else TOK

        def scores_tensor(h):
            e = h.e
            if e >= 2:
                nc.tensor.wait_ge(negmax_ready, e - 1)
            if h.wait_tensor:
                h.wait_tensor()
            for t in range(TT):
                n = h.keys(t)
                to = ps[:, e % 2, t * TOK:t * TOK + n]
                last = nc.tensor.matmul(to, h.q(t), h.k(n), start=True, stop=h.extra is None, skip_group_check=True)
                if h.extra:
                    last = nc.tensor.matmul(to, h.extra[0], h.extra[1](n), start=False, stop=True, skip_group_check=True)
            last.then_inc(scores_psum, 1)

        def turn_tensor(h):
            e = h.e
            nc.tensor.wait_ge(prob_ready, e + 1)
            if e >= 2:
                nc.tensor.wait_ge(turned_ready, e - 1)
            for s in range(TT):
                for t in range(s if h.causal else 0, TT):
                    col = s * TOK + t * P - (s * P if h.causal else 0)
                    last = nc.tensor.transpose(ps[:, 2 + e % 2, col:col + P],
                                               prob[:, e % 2, t * TOK + s * P:t * TOK + (s + 1) * P], ident[:, :])
            last.then_inc(turned_psum, 1)

        def values_tensor(h):
            e = h.e
            pair = e // 2
            nc.tensor.wait_ge(turned_ready, e + 1)
            if e % 2 == 0 and pair >= 2:
                nc.tensor.wait_ge(o_lo_ready, pair - 1)
            q0 = P if h.causal else 0
            to = ps[h.row:h.row + HD, 4 + pair % 2, :]
            nc.tensor.matmul(to[:, 0:TOK], h.v(0), prob_t[:, e % 2, 0:TOK], start=True, stop=False, skip_group_check=True)
            nc.tensor.matmul(to[:, q0:TOK], h.v(1), prob_t[:, e % 2, TOK:2 * TOK - q0], start=False, stop=True,
                             skip_group_check=True).then_inc(o_psum, 1)

        def attention_tensor(heads, between=None):
            for n in range(len(heads) + 2):
                if n < len(heads):
                    scores_tensor(heads[n])
                if 1 <= n <= len(heads):
                    turn_tensor(heads[n - 1])
                if n >= 2:
                    values_tensor(heads[n - 2])
                if between:
                    between(n)

        def exp_scalar(h):
            e = h.e
            nc.scalar.wait_ge(negmax_ready, e + 1)
            for t in range(TT):
                sc = prob[:, e % 2, t * TOK:t * TOK + h.keys(t)]
                last = nc.scalar.activation(sc, sc, ACT.Exp, bias=nmx[:, e % 2, t:t + 1], accum_out=den[:, e % 2, t:t + 1])
            if h.sink is not None:
                last = nc.scalar.activation(sink_e[:, e % 2, :], nmx[:, e % 2, :], ACT.Exp, bias=h.sink)
            last.then_inc(exp_ready, 1)

        def turned_scalar(h):
            e = h.e
            nc.scalar.wait_ge(turned_psum, e + 1)
            if e >= 2:
                nc.scalar.wait_ge(o_psum, e - 1)
            n = 3 * P if h.causal else 4 * P
            nc.scalar.copy(prob_t[:, e % 2, 0:n], ps[:, 2 + e % 2, 0:n]).then_inc(turned_ready, 1)

        def out_scalar(h):
            nc.scalar.wait_ge(o_psum, h.e + 1)
            nc.scalar.copy(h_hi[:, h.tile, :], ps[:, 4 + h.e // 2 % 2, 0:TOK]).then_inc(o_hi_ready, 1)

        def attention_scalar(heads, between=None):
            for n in range(len(heads) + 2):
                if n < len(heads):
                    exp_scalar(heads[n])
                if 1 <= n <= len(heads):
                    turned_scalar(heads[n - 1])
                if n >= 2 and n % 2:
                    out_scalar(heads[n - 2])
                if between:
                    between(n)

        def max_vector(h):
            e = h.e
            nc.vector.wait_ge(scores_psum, e + 1)
            if e >= 2:
                nc.vector.wait_ge(turned_psum, e - 1)
            if h.wait_vector:
                h.wait_vector()
            for t in range(TT):
                n = h.keys(t)
                last = nc.vector.tensor_tensor_reduce(prob[:, e % 2, t * TOK:t * TOK + n], ps[:, e % 2, t * TOK:t * TOK + n],
                                                      h.mask(t), h.scale(t), -3.0e38, ALU.add, ALU.max,
                                                      mx[:, e % 2, t:t + 1])
            dve_then(last)
            floor = -3.0e38 if h.sink is None else h.sink
            nc.vector.tensor_scalar(nmx[:, e % 2, :], mx[:, e % 2, :], floor, -1.0, ALU.max, ALU.mult).then_inc(negmax_ready, 1)

        def prob_vector(h):
            e = h.e
            nc.vector.wait_ge(exp_ready, e + 1)
            if h.sink is not None:
                dve_then(nc.vector.tensor_tensor(den[:, e % 2, :], den[:, e % 2, :], sink_e[:, e % 2, :], ALU.add))
            dve_then(nc.vector.reciprocal(rden[:, e % 2, :], den[:, e % 2, :]))
            for t in range(TT):
                sc = prob[:, e % 2, t * TOK:t * TOK + h.keys(t)]
                last = nc.vector.tensor_scalar(sc, sc, rden[:, e % 2, t:t + 1], None, ALU.mult)
            last.then_inc(prob_ready, 1)

        def out_vector(h):
            pair = h.e // 2
            nc.vector.wait_ge(o_hi_ready, pair + 1)
            nc.vector.tensor_tensor(h_lo[:, h.tile, :], ps[:, 4 + pair % 2, 0:TOK], h_hi[:, h.tile, :].bitcast(F32),
                                    ALU.subtract).then_inc(o_lo_ready, 1)

        def attention_vector(heads, between=None):
            for n in range(len(heads) + 2):
                if n < len(heads):
                    max_vector(heads[n])
                if 1 <= n <= len(heads):
                    prob_vector(heads[n - 1])
                if n >= 2 and n % 2:
                    out_vector(heads[n - 2])
                if between:
                    between(n)

        G, H1, HM = 6, 6, 4
        mem = carve(0, TT, D)
        uv = carve(0, TT, 768)
        fqk = carve(1536, 6, TOK)
        fv = carve(3072, TT, 390)
        mq = carve(3852, 2, TOK)
        km = carve(4364, 2, TOK)
        vm = carve(4876, TT, 256)
        ws = carve(5388, G, P)
        oa = carve(5388, TT, 384)
        ws_t = carve(6156, G, P)
        sel = arena[0:6, 6924:7692].rearrange("p (h c) -> p h c", h=H1)
        nct = arena[0:6, 7692:7948]
        vgain = carve(7948, 384)
        bs = arena[0:6, 8332:8460]
        ssv, rsv = small[:, 0:12], small[:, 12:24]
        gz, gaz, gmin, ge, lf = (small[:, 24 + 12 * n:36 + 12 * n].rearrange("p (t h) -> p t h", t=TT) for n in range(5))
        bs_t = small[:, 84:90]
        bf = small[:, 90:96]
        g1 = act[:, :, :].rearrange("p a b -> p (a b)")
        small_landed = sem("small_landed")
        bf_landed = sem("bf_landed")
        vgain_landed = sem("vgain_landed")
        ws_ready = sem("ws_ready")
        proj_out = sem("proj_out")
        gelu_in = sem("gelu_in")
        gelu_tanh = sem("gelu_tanh")
        v_ready = sem("v_ready")
        gate_in = sem("gate_in")
        gate_log = sem("gate_log")
        lf_ready = sem("lf_ready")
        ws_psum = sem("ws_psum")
        ws_t_ready = sem("ws_t_ready")
        ct_psum = sem("ct_psum")
        nct_ready = sem("nct_ready")
        mixed_psum = sem("mixed_psum")
        oa_ready = sem("oa_ready")
        oa_psum = sem("oa_psum")
        oa_hi = sem("oa_hi")
        oa_lo = sem("oa_lo")
        PROJ_TO = [km, vm, uv[:, :, 0:256], uv[:, :, 256:512], uv[:, :, 512:768], fqk[:, 0:2, :], fqk[:, 2:4, :],
                   fqk[:, 4:6, :], fv[:, :, 0:256], fv[:, :, 256:390], mq]
        PROJ_FEATURES = {0, 5, 6, 7, 10}

        def head_fox(h):
            r = (h % 2) * HD
            return Head(h, lambda t: fqk[r:r + HD, h // 2, t * P:(t + 1) * P], lambda n: fqk[r:r + HD, 3 + h // 2, 0:n],
                        lambda s: fv[:, s, h * HD:(h + 1) * HD], lambda t: causal[:, 2 * P - t * P:3 * P],
                        lambda t: 0.125, 3 + h // 2, r, extra=(sel[:, h, :], lambda n: nct[:, 0:n]))

        def head_mem(h):
            r = (h % 2) * HD
            return Head(H1 + h, lambda t: mq[r:r + HD, h // 2, t * P:(t + 1) * P], lambda n: km[r:r + HD, h // 2, 0:n],
                        lambda s: vm[:, s, h * HD:(h + 1) * HD], lambda t: causal[:, 0:2 * P],
                        lambda t: 0.125, 6 + h // 2, r, causal=False)

        heads_m1 = [head_fox(h) for h in range(H1)] + [head_mem(h) for h in range(HM)]

        NBK, AH = 32, 16
        PAIRS = 1024
        CHUNKS = 64 * P // PAIRS
        window = arena[:, 9676:9868].bitcast(I32)
        table = arena[:, 9868:9996]
        table_hi, table_lo = act_lo[:, 0, 0:P], act_lo[:, 0, P:2 * P]
        edges = keep[:, 532:534]
        dist = scratch[:, 0:PAIRS].bitcast(I32)
        above = scratch[:, PAIRS:2 * PAIRS]
        hot = act_hi[:, :, :].rearrange("p a b -> p (a b)")[:, 0:PAIRS]
        staged = junk
        PITCH = 2 * P
        canvas = nc.dram_tensor("canvas", (AH, TT, P * (PITCH + 1) + 128), F32, kind="Internal").ap()
        rows = canvas[:, :, 0:P * PITCH].rearrange("h n (t s) -> h n t s", s=PITCH)
        skewed = canvas[:, :, 1:1 + P * (PITCH + 1)].rearrange("h n (t s) -> h n t s", s=PITCH + 1)
        window_landed = sem("window_landed")
        window_zero = sem("window_zero")
        table_zero = sem("table_zero")
        table_landed = sem("table_landed")
        table_hi_ready = sem("table_hi_ready")
        table_ready = sem("table_ready")
        neg_ready = sem("neg_ready")
        canvas_filled = sem("canvas_filled")
        canvas_written = sem("canvas_written")
        dist_ready = sem("dist_ready")
        hot_ready = sem("hot_ready")
        bias_psum = sem("bias_psum")
        bias_out = sem("bias_out")

        def dist_pool(c):
            nc.gpsimd.wait_ge(hot_ready, c) if c else nc.gpsimd.wait_ge(h_psum, 8)
            w = window[:, 8 * c:8 * c + 8]
            key = bass.AP(tensor=w.tensor, offset=w.offset, ap=[list(w.ap[0]), [1, 8], [1, P]])
            query = window[:, 127 + 8 * c:135 + 8 * c].unsqueeze(2).to_broadcast([P, 8, P])
            nc.gpsimd.tensor_tensor(dist.rearrange("p (j u) -> p j u", j=8), query, key, ALU.subtract).then_inc(dist_ready, 1)

        def hot_vector(c):
            nc.vector.wait_ge(dist_ready, c + 1)
            if c:
                nc.vector.wait_ge(bias_psum, c)
            dve_then(nc.vector.tensor_scalar(above, dist, edges[:, 0:1], None, ALU.is_ge))
            nc.vector.scalar_tensor_tensor(hot, dist, edges[:, 1:2], above, ALU.is_lt, ALU.mult).then_inc(hot_ready, 1)

        def bias_tensor(c):
            nc.tensor.wait_ge(hot_ready, c + 1)
            if c >= 2:
                nc.tensor.wait_ge(bias_out, c - 1)
            for half in range(2):
                to, marks = ps[:, 2 * (c % 2) + half, :], hot[:, half * 512:(half + 1) * 512]
                nc.tensor.matmul(to, table_hi, marks, start=True, stop=False, skip_group_check=True)
                last = nc.tensor.matmul(to, table_lo, marks, start=False, stop=True, skip_group_check=True)
            last.then_inc(bias_psum, 1)

        def bias_scalar(c):
            nc.scalar.wait_ge(bias_psum, c + 1)
            if c:
                nc.scalar.wait_ge(canvas_written, 64 * c)
            nc.scalar.copy(staged[0:64, :], ps[0:64, 2 * (c % 2):2 * (c % 2) + 2, :].rearrange("p b c -> p (b c)")).then_inc(bias_out, 1)

        def bias_store(c):
            nc.gpsimd.wait_ge(bias_out, c + 1)
            for g in range(4):
                t0 = g % 2 * 64 + 8 * c
                nc.gpsimd.dma_start(skewed[:, g // 2, t0:t0 + 8, 0:P],
                                    staged[g * AH:(g + 1) * AH, :].rearrange("h (t u) -> h t u", t=8)).then_inc(canvas_written, 16)

        qa = carve(0, TT, D)
        kva = carve(2048, TT, 256)
        kd = carve(2560, TT, 256)
        qt_a = carve(3072, 8, TOK)
        kt_a = carve(5120, 2, TOK)
        BR = 6
        bias = carve(5632, BR, 3 * P)
        sq_a = scratch[:, 0:1024].rearrange("p (b c) -> p b c", b=2)
        ss_a, rs_a = small[:, 0:40], small[:, 40:80]
        q_col, k_col = keep[:, 514:515], keep[:, 515:516]
        sinks = keep[:, 516:532]
        a_small = sem("a_small")
        a_out_ready = sem("a_out_ready")
        a_squares = sem("a_squares")
        a_sums = sem("a_sums")
        a_rstd = sem("a_rstd")
        a_scaled = sem("a_scaled")
        a_turned = sem("a_turned")
        a_turned_out = sem("a_turned_out")
        q_col_ready = sem("q_col_ready")
        bias_landed = [sem(f"bias_landed{n}") for n in range(BR)]
        E_A = len(heads_m1)

        def bias_load(h):
            if h >= BR:
                nc.gpsimd.wait_ge(negmax_ready, E_A + h - BR + 1)
            nc.gpsimd.dma_start(bias[:, h % BR, 0:P], rows[h, 0, :, P:2 * P]).then_inc(bias_landed[h % BR], 16)
            nc.gpsimd.dma_start(bias[:, h % BR, P:3 * P], rows[h, 1, :, :]).then_inc(bias_landed[h % BR], 16)

        def head_a(h):
            r = (h % 2) * HD
            g = h // 8
            return Head(E_A + h, lambda t: qt_a[r:r + HD, h // 2, t * P:(t + 1) * P], lambda n: kt_a[r:r + HD, g, 0:n],
                        lambda s: kva[:, s, P + g * HD:P + (g + 1) * HD],
                        lambda t: bias[:, h % BR, t * P:3 * P if t else P], lambda t: 1.0, h // 2, r, sink=sinks[:, h:h + 1],
                        wait_vector=lambda: nc.vector.wait_ge(bias_landed[h % BR], 32 * (h // BR + 1)))

        heads_a = [head_a(h) for h in range(AH)]

        BH, QK = 16, 96
        qb = carve(0, TT, BH * QK)
        kvb = carve(3072, TT, BH * P)
        qk_t = arena[0:QK, 7168:8192].rearrange("p (b c) -> p b c", b=2)
        c_gain = carve(8192, 384)
        cb = act[:, :, :].rearrange("p a b -> p (a b)")[:, 0:832].rearrange("p (t c) -> p t c", t=TT)
        cn = scratch[:, 0:768].rearrange("p (t c) -> p t c", t=TT)
        kc = scratch[:, :].rearrange("p (t h d) -> p t h d", t=TT, h=BH)
        ss_q, ss_k, rs_q, rs_k = (small[:, 32 * n:32 * n + 32] for n in range(4))
        ss_c, rs_c = sums[:, 48:54], rstd[:, 48:52]
        cos, sin = (keep[:, 32 * n:32 * n + 32].rearrange("p (t c) -> p t c", t=TT) for n in range(2))
        gq, gk = keep[:, 64:160], keep[:, 160:256]
        qb_col, kb_col = keep[0:QK, 512:513], keep[0:QK, 513:514]
        rot = {name: keep[:, 256 + 32 * n:288 + 32 * n].rearrange("p (t c) -> p t c", t=TT)
               for n, name in enumerate(("q1c", "q2s", "q2c", "q1s", "k1c", "k2s", "k2c", "k1s"))}
        rope_at = [carve(3072 + 32 * n, TT, 16) for n in range(6)]
        pos_i = arena[:, 3264:3266].bitcast(I32)
        pos_f = arena[:, 3266:3268]
        freq = arena[:, 3268:3284]
        b_small = sem("b_small")
        pos_landed = sem("pos_landed")
        angle_ready = sem("angle_ready")
        sin_ready = sem("sin_ready")
        rot_ready = sem("rot_ready")
        c_out = sem("c_out")
        c_squares = sem("c_squares")
        c_rstd = sem("c_rstd")
        cn_ready = sem("cn_ready")
        c_turned = sem("c_turned")
        c_hi = sem("c_hi")
        c_lo = sem("c_lo")
        up_scalar = sem("up_scalar")
        up_vector = sem("up_vector")
        q_squares = sem("q_squares")
        q_sums = sem("q_sums")
        k_squares = sem("k_squares")
        k_sums = sem("k_sums")
        qk_rstd = sem("qk_rstd")
        q_roped = sem("q_roped")
        kc_ready = sem("kc_ready")
        qk_psum = sem("qk_psum")
        qk_q_out = sem("qk_q_out")
        qk_k_out = sem("qk_k_out")
        E_B = E_A + AH

        def head_b(h):
            def wait_tensor():
                nc.tensor.wait_ge(qk_q_out, h + 1)
                nc.tensor.wait_ge(qk_k_out, h + 1)
            return Head(E_B + h, lambda t: qk_t[:, h % 2, t * P:(t + 1) * P], lambda n: qk_t[:, h % 2, TOK:TOK + n],
                        lambda s: kvb[:, s, h * P + HD:(h + 1) * P], lambda t: causal[:, 2 * P - t * P:3 * P],
                        lambda t: rs_q[:, t * BH + h:t * BH + h + 1], h // 2, (h % 2) * HD,
                        wait_tensor=wait_tensor)

        heads_b = [head_b(h) for h in range(BH)]

        def turn_qk_tensor(h):
            if h >= BH:
                return
            if h >= 2:
                nc.tensor.wait_ge(qk_q_out, h - 1)
                nc.tensor.wait_ge(qk_k_out, h - 1)
            for t in range(TT):
                nc.tensor.transpose(ps[0:QK, 6 + h % 2, t * P:(t + 1) * P], qb[:, t, h * QK:(h + 1) * QK], ident[:, :])
                last = nc.tensor.transpose(ps[0:QK, 6 + h % 2, TOK + t * P:TOK + (t + 1) * P], kc[:, t, h, :], ident[:, :])
            last.then_inc(qk_psum, 1)

        def turned_q_scalar(h):
            if h >= BH:
                return
            nc.scalar.wait_ge(qk_psum, h + 1)
            if h >= 2:
                nc.scalar.wait_ge(scores_psum, E_B + h - 1)
            nc.scalar.activation(qk_t[:, h % 2, 0:TOK], ps[0:QK, 6 + h % 2, 0:TOK], ACT.Copy, scale=qb_col).then_inc(qk_q_out, 1)

        def turned_k_vector(h):
            if h >= BH:
                return
            nc.vector.wait_ge(qk_q_out, h + 1)
            nc.vector.tensor_scalar(qk_t[:, h % 2, TOK:2 * TOK], ps[0:QK, 6 + h % 2, TOK:2 * TOK], kb_col, None, ALU.mult).then_inc(qk_k_out, 1)

        tanh_ready = {st: sem(f"tanh_ready_{st}") for st in swiglu}
        half_ready = {st: sem(f"half_ready_{st}") for st in swiglu}
        hidden_ready = {st: sem(f"hidden_ready_{st}") for st in ("F0", "F1", "F2", "F3", "F4")}
        hidden_hi = {st: sem(f"hidden_hi_{st}") for st in hidden_ready}
        hidden_lo = {st: sem(f"hidden_lo_{st}") for st in hidden_ready}
        tanh_g = carve(0, 2, 512)
        half_g = carve(1024, 2, 512)

        def hidden_bank(bank):
            return lambda f: ps[:, bank, f * TOK:(f + 1) * TOK]

        def second_product(st, b, s, buf, begin, end, turn=0, per=0):
            nc.tensor.wait_ge(hidden_lo[st], s + 1 + per * turn)
            nc.tensor.wait_ge(lo_ready, b + 1 + RAW * turn)
            hi, lo = parts(b)
            for f in range(2):
                for t in range(TT):
                    c = f * TOK + t * P
                    still = act_hi[:, buf, c:c + P], act_lo[:, buf, c:c + P]
                    for half in range(2):
                        cols = slice(half * 512, (half + 1) * 512)
                        last = product(ps[:, 4 + 2 * t + half, :], still, (hi[:, f, cols], lo[:, f, cols]),
                                       begin and f == 0, end and f == 1)
            last.then_inc(block_used, 1)

        def round_hidden(st, s, buf, down_block, turn=0, per=0):
            nc.scalar.wait_ge(hidden_ready[st], s + 1 + per * turn)
            if down_block is not None:
                nc.scalar.wait_ge(block_used, down_block + 1 + RAW * turn)
            nc.scalar.copy(act_hi[:, buf, :], act[:, buf, :]).then_inc(hidden_hi[st], 1)

        def split_hidden(st, s, buf, turn=0, per=0):
            nc.vector.wait_ge(hidden_hi[st], s + 1 + per * turn)
            nc.vector.tensor_tensor(act_lo[:, buf, :], act[:, buf, :], act_hi[:, buf, :].bitcast(F32),
                                    ALU.subtract).then_inc(hidden_lo[st], 1)

        def b_up(s):
            return first["F0"] + (2 * s - 1 if s else 0)

        def b_down(s):
            return first["F0"] + (2 * s + 2 if s < I0 - 1 else 2 * s + 1)

        def relu_tensor(s, turn=0):
            if s >= 3:
                nc.tensor.wait_ge(hidden_ready["F0"], s - 2 + 3 * turn)
            features_out(b_up(s), hidden_bank(s % 3), turn=turn, wait_h=8 if s == 0 else None)
            if s:
                second_product("F0", b_down(s - 1), s - 1, (s - 1) % 3, s == 1, False, turn, 3)

        relu_ready = sem("relu_ready")
        positive = carve(0, 3, 512)

        def relu_scalar(s, turn=0):
            nc.scalar.wait_ge(block_used, b_up(s) + 1 + RAW * turn)
            nc.scalar.activation(positive[:, s % 3, :], ps[:, s % 3, :], ACT.Relu).then_inc(relu_ready, 1)
            round_hidden("F0", s, s % 3, b_down(s - 3) if s >= 3 else None, turn, 3)
            if s:
                round_block(b_up(s) + 3, turn)
                round_block(b_up(s) + 4, turn)
            else:
                round_block(b_up(0) + 3)

        def relu_vector(s, turn=0):
            nc.vector.wait_ge(relu_ready, s + 1 + 3 * turn)
            nc.vector.tensor_tensor(act[:, s % 3, :], positive[:, s % 3, :], ps[:, s % 3, :], ALU.mult).then_inc(hidden_ready["F0"], 1)
            if s:
                split_block(b_up(s) + 3, turn)
            split_hidden("F0", s, s % 3, turn, 3)
            split_block(b_up(s) + (4 if s else 3), turn)

        def up_source(s):
            return i["w_ff1"][0].rearrange("(k p) n -> p k n", p=P)[:, :, bass.ds(256 * s, 256)]

        def rows_source(w, s):
            return w.rearrange("(s k p) n -> p s k n", k=2, p=P)[:, bass.ds(s, 1)].rearrange("p s k n -> p (s k) n")

        def relu_load(s, turn=0):
            load(b_up(s), up_source(s + 3 * turn), turn)
            if s:
                load(b_down(s - 1), rows_source(i["w_ff2"][0], s - 1 + 3 * turn), turn)

        RELU_PEEL = 4

        def relu_steps(engine, step):
            for s in range(RELU_PEEL):
                step(s)
            with engine.Fori(0, (I0 - RELU_PEEL) // 3) as turn:
                for s in range(RELU_PEEL, RELU_PEEL + 3):
                    step(s, turn)

        def b_gate(st, s):
            return first[st] + (3 * s - 1 if s else 0)

        def b_upper(st, s):
            return first[st] + (3 * s if s else 1)

        def b_lower(st, s):
            return first[st] + (3 * s + 4 if s < I1 - 1 else 3 * s + 2)

        def column_source(w, s):
            return w.rearrange("(k p) n -> p k n", p=P)[:, :, bass.ds(256 * s, 256)]

        def swiglu_load(st, s, turn=0):
            wg, wu, wd = swiglu_weights(st)
            load(b_gate(st, s), column_source(wg, s + 2 * turn), turn)
            load(b_upper(st, s), column_source(wu, s + 2 * turn), turn)
            if s:
                load(b_lower(st, s - 1), rows_source(wd, s - 1 + 2 * turn), turn)

        def swiglu_tensor(st, n, s, turn=0):
            if s >= 2:
                nc.tensor.wait_ge(hidden_ready[st], s - 1 + 2 * turn)
            features_out(b_gate(st, s), hidden_bank(s % 2), turn=turn, wait_h=4 * n if s == 0 else None)
            features_out(b_upper(st, s), hidden_bank(2 + s % 2), turn=turn)
            if s:
                second_product(st, b_lower(st, s - 1), s - 1, (s - 1) % 2, s == 1, False, turn, 2)

        def swiglu_scalar(st, s, turn=0):
            nc.scalar.wait_ge(block_used, b_gate(st, s) + 1 + RAW * turn)
            nc.scalar.activation(tanh_g[:, s % 2, :], ps[:, s % 2, :], ACT.Tanh, scale=0.5).then_inc(tanh_ready[st], 1)
            round_block(b_gate(st, s) + 3, turn)
            round_block(b_upper(st, s) + 3, turn)
            round_hidden(st, s, s % 2, b_lower(st, s - 2) if s >= 2 else None, turn, 2)
            if s:
                round_block(b_upper(st, s) + 4, turn)

        def swiglu_vector(st, s, turn=0):
            nc.vector.wait_ge(tanh_ready[st], s + 1 + 2 * turn)
            nc.vector.scalar_tensor_tensor(half_g[:, s % 2, :], tanh_g[:, s % 2, :], 1.0, ps[:, s % 2, :],
                                           ALU.add, ALU.mult).then_inc(half_ready[st], 1)
            split_block(b_gate(st, s) + 3, turn)
            nc.vector.wait_ge(block_used, b_upper(st, s) + 1 + RAW * turn)
            nc.vector.wait_ge(half_ready[st], s + 1 + 2 * turn)
            nc.vector.scalar_tensor_tensor(act[:, s % 2, :], half_g[:, s % 2, :], 0.5, ps[:, 2 + s % 2, :],
                                           ALU.mult, ALU.mult).then_inc(hidden_ready[st], 1)
            split_block(b_upper(st, s) + 3, turn)
            split_hidden(st, s, s % 2, turn, 2)
            if s:
                split_block(b_upper(st, s) + 4, turn)

        SWIGLU_PEEL = 3

        def swiglu_steps(engine, st, step):
            alone = 2 if st == "F4" or st == STAGES[-1] else 0
            for s in range(SWIGLU_PEEL):
                step(st, s)
            with engine.Fori(0, (I1 - SWIGLU_PEEL - alone) // 2) as turn:
                for s in range(SWIGLU_PEEL, SWIGLU_PEEL + 2):
                    step(st, s, turn)
            for s in range(I1 - alone, I1):
                step(st, s)

        block = ctx.enter_context(nc.Block())

        @block.gpsimd
        def _(pool):
            pool_then(nc.gpsimd.memset(ident[:, :], 1.0))
            pool_then(nc.gpsimd.affine_select(out=ident[:, :], in_=ident[:, :], compare_op=ALU.is_equal, fill=0.0,
                                              base=0, pattern=[[-1, P]], channel_multiplier=1))
            pool_then(nc.gpsimd.memset(tri[:, 0:P], 0.0))
            pool_then(nc.gpsimd.memset(tri[:, P:3 * P], 1.0))
            pool_then(nc.gpsimd.affine_select(out=tri[:, P:2 * P], in_=tri[:, P:2 * P], compare_op=ALU.is_ge, fill=0.0,
                                              base=0, pattern=[[1, P]], channel_multiplier=-1))
            pool_then(nc.gpsimd.memset(causal[:, :], 0.0))
            nc.gpsimd.affine_select(out=causal[:, 2 * P:3 * P], in_=causal[:, 2 * P:3 * P], compare_op=ALU.is_ge, fill=NEG,
                                    base=0, pattern=[[-1, P]], channel_multiplier=1).then_inc(tables_ready, 1)
            pool_then(nc.gpsimd.memset(halves[:, :], -0.5))
            nc.gpsimd.dma_start(pos_i, i["positions_2"].rearrange("a (t p) -> p (a t)", p=P), allow_slow_non_contiguous=True).then_inc(pos_landed, 16)
            nc.gpsimd.dma_start(freq, i["rope_freq"].to_broadcast([P, 16])).then_inc(pos_landed, 16)
            nc.gpsimd.dma_start(gq, i["b_q_gain_2"][0:1, :].to_broadcast([P, QK])).then_inc(pos_landed, 16)
            nc.gpsimd.dma_start(gk, i["b_k_gain_2"][0:1, :].to_broadcast([P, QK])).then_inc(pos_landed, 16)
            norm_pool(0)
            norm_pool(1)
            nc.gpsimd.memset(window, 0).then_inc(window_zero, 1)
            nc.gpsimd.memset(table, 0.0).then_inc(table_zero, 1)
            pool.wait_ge(window_zero, 1)
            for g in range(4):
                skip = max(0, 127 - 64 * g)
                n = 191 - skip
                s0 = 64 * g - 127 + skip
                nc.gpsimd.dma_start(window[g * NBK:(g + 1) * NBK, skip:191],
                                    i["positions_2"][0:1, s0:s0 + n].to_broadcast([NBK, n])).then_inc(window_landed, 16)
            pool.wait_ge(table_zero, 1)
            for g in range(4):
                nc.gpsimd.dma_start(table[g * NBK:(g + 1) * NBK, g * AH:(g + 1) * AH], i["rel_bias_2"]).then_inc(table_landed, 16)
            nc.gpsimd.dma_start(edges, i["bucket_edges"]).then_inc(table_landed, 16)
            nc.gpsimd.dma_start(ws, i["gmlp_w_s"][0].rearrange("g t s -> t g s")).then_inc(small_landed, 16)
            nc.gpsimd.dma_start(bs, i["gmlp_b_s"][0]).then_inc(small_landed, 16)
            nc.gpsimd.dma_start(bf, i["b_forget"][0:1, :].to_broadcast([P, H1])).then_inc(bf_landed, 16)
            nc.gpsimd.dma_start(vgain, i["gmlp_v_norm"][0:1, :].to_broadcast([P, 384])).then_inc(vgain_landed, 16)
            pool_then(nc.gpsimd.memset(sel[:, :, :], 1.0))
            nc.gpsimd.affine_select(out=sel[:, :, :], in_=sel[:, :, :], compare_op=ALU.is_equal, fill=0.0,
                                    base=0, pattern=[[-1, H1], [0, P]], channel_multiplier=1).then_inc(tables_ready, 1)
            pool.wait_ge(small_landed, 32)
            nc.gpsimd.affine_select(out=ws, in_=ws, compare_op=ALU.is_ge, fill=0.0,
                                    base=0, pattern=[[0, G], [-1, P]], channel_multiplier=1).then_inc(ws_ready, 1)
            nc.gpsimd.memset(act[:, :, :], NEG).then_inc(neg_ready, 1)
            pool.wait_ge(neg_ready, 1)
            fill = canvas.rearrange("h n c -> (h n c)").rearrange("(p c) -> p c", p=P)
            NF = fill.shape[1] // 6
            for n in range(6):
                nc.gpsimd.dma_start(fill[:, n * NF:(n + 1) * NF],
                                    act[:, :, :].rearrange("p a b -> p (a b)")[:, 0:NF]).then_inc(canvas_filled, 16)
            pool.wait_ge(window_landed, 64)
            dist_pool(0)
            pool.wait_ge(canvas_filled, 96)
            for c in range(CHUNKS):
                if c + 1 < CHUNKS:
                    dist_pool(c + 1)
                bias_store(c)
            pool.wait_ge(v_sumsq, 1)
            rsqrt_pool(rsv, ssv, HD, v_rstd)
            add_normed_pool(0)
            if "F0" in STAGES:
                norm_pool(2)
                add_normed_pool(1)
            if "F1" in STAGES:
                norm_pool(3)
            if "MA" in STAGES:
                pool.wait_ge(x_ready, 2)
                nc.gpsimd.dma_start(sinks, i["a_sinks_2"][0:1, :].to_broadcast([P, AH])).then_inc(a_small, 16)
                for r in range(2):
                    rows_of = slice(r * HD, (r + 1) * HD)
                    nc.gpsimd.dma_start(q_col[rows_of, :], i["a_q_gain_2"].rearrange("a n -> n a"), allow_slow_non_contiguous=True).then_inc(a_small, 16)
                    nc.gpsimd.dma_start(k_col[rows_of, :], i["a_k_gain_2"].rearrange("a n -> n a"), allow_slow_non_contiguous=True).then_inc(a_small, 16)
                pool.wait_ge(canvas_written, 64 * CHUNKS)
                for h in range(BR):
                    bias_load(h)
                norm_pool(4)
                for p in range(5):
                    pool.wait_ge(a_sums, p + 1)
                    rsqrt_pool(rs_a[:, 8 * p:8 * p + 8], ss_a[:, 8 * p:8 * p + 8], HD, a_rstd)
                for h in range(BR, AH):
                    bias_load(h)
            if "F2" in STAGES:
                norm_pool(5)
            if "F3" in STAGES:
                norm_pool(6)
            if "MB" in STAGES:
                pool_then(nc.gpsimd.memset(qb_col, 1.0))
                pool_then(nc.gpsimd.memset(kb_col, 1.0))
                nc.gpsimd.dma_start(qb_col[0:HD, :], i["b_q_gain_2"][:, 0:HD].rearrange("a n -> n a"), allow_slow_non_contiguous=True).then_inc(b_small, 16)
                nc.gpsimd.dma_start(kb_col[0:HD, :], i["b_k_gain_2"][:, 0:HD].rearrange("a n -> n a"), allow_slow_non_contiguous=True).then_inc(b_small, 16)
                pool.wait_ge(x_ready, 8)
                nc.gpsimd.dma_start(c_gain[:, 0:256], i["b_q_norm_2"].to_broadcast([P, 256])).then_inc(b_small, 16)
                nc.gpsimd.dma_start(c_gain[:, 256:384], i["b_kv_norm_2"].to_broadcast([P, P])).then_inc(b_small, 16)
                norm_pool(7)
                pool.wait_ge(c_squares, 6)
                rsqrt_pool(rs_c[:, 0:2], ss_c[:, 0:2], 256, c_rstd)
                rsqrt_pool(rs_c[:, 2:4], ss_c[:, 2:4], P, c_rstd)
                pool.wait_ge(q_squares, 2)
                pool.wait_ge(rot_ready, 1)
                roped = [act[:, 2, n * 256:n * 256 + 256].rearrange("p (h c) -> p h c", h=BH) for n in range(2)]
                for t in range(TT):
                    q1 = qb[:, t, :].rearrange("p (h d) -> p h d", h=BH)[:, :, HD:HD + 16]
                    q2 = qb[:, t, :].rearrange("p (h d) -> p h d", h=BH)[:, :, HD + 16:QK]

                    def turn(name):
                        return rot[name][:, t, :].unsqueeze(1).to_broadcast([P, BH, 16])

                    a, b = roped[0], roped[1]
                    nc.gpsimd.tensor_tensor(a, q1, turn("q1s"), ALU.mult)
                    pool_then(nc.gpsimd.tensor_tensor(b, q2, turn("q2s"), ALU.mult))
                    pool_then(nc.gpsimd.tensor_tensor(q1, q1, turn("q1c"), ALU.mult))
                    nc.gpsimd.tensor_tensor(q1, q1, b, ALU.subtract)
                    pool_then(nc.gpsimd.tensor_tensor(q2, q2, turn("q2c"), ALU.mult))
                    last = nc.gpsimd.tensor_tensor(q2, q2, a, ALU.add)
                    if t == 0:
                        pool_then(last)
                last.then_inc(q_roped, 1)
                pool.wait_ge(q_sums, 1)
                rsqrt_pool(rs_q, ss_q, 1, qk_rstd, eps=QK * EPS)
                pool.wait_ge(k_sums, 1)
                rsqrt_pool(rs_k, ss_k, QK, qk_rstd)
            if "F4" in STAGES:
                norm_pool(8)

        @block.sync
        def _(sp):
            sp.dma_start(mem, i["mem"][0].rearrange("(t p) d -> p t d", p=P)).then_inc(mem_landed, 16)

            def load_gain(g):
                sp.dma_start(gain[:, g % GS, :], gains[g].rearrange("(a n) -> a n", a=1).to_broadcast([P, D])).then_inc(gain_landed[g % GS], 16)

            load_gain(0)
            sp.dma_start(x[:, :, :], i["x"][0].rearrange("(t p) d -> p t d", p=P)).then_inc(x_landed, 16)
            load_gain(1)
            for b in range(first["F0"]):
                load(b)
                if b == 8:
                    sp.wait_ge(xn_ready, 4)
                    load_gain(2)
                    load_gain(3)
            if "F0" in STAGES:
                relu_steps(sp, relu_load)
                load(b_down(I0 - 1))
                sp.wait_ge(x_ready, 2)
                load_gain(4)
                sp.wait_ge(xn_ready, 6)
                load_gain(5)
            if "F1" in STAGES:
                swiglu_steps(sp, "F1", swiglu_load)
                load(b_lower("F1", I1 - 1))

            def next_gain(g, used, count):
                sp.wait_ge(used, count)
                load_gain(g)

            if "MA" in STAGES:
                next_gain(6, x_ready, 4)
                next_gain(7, xn_ready, 8)
                for b in range(first["a_in"], first["a_out"] + 4):
                    load(b)
            if "F2" in STAGES:
                swiglu_steps(sp, "F2", swiglu_load)
                load(b_lower("F2", I1 - 1))
                next_gain(8, xn_ready, 10)
                swiglu_steps(sp, "F3", swiglu_load)
                load(b_lower("F3", I1 - 1))
                next_gain(9, xn_ready, 12)
            if "MB" in STAGES:
                for b in range(first["b_in"], first["b_out"] + 4):
                    load(b)
                next_gain(10, xn_ready, 14)
            if "F4" in STAGES:
                swiglu_steps(sp, "F4", swiglu_load)
                load(b_lower("F4", I1 - 1))
            for t in range(TT):
                sp.wait_ge(x_ready, 2 * (len(STAGES) - 1) + t + 1)
                sp.dma_start(out[t * P:(t + 1) * P, :], x[:, t, :]).then_inc(out_landed, 16)
            sp.wait_ge(out_landed, 32)

        @block.scalar
        def _(scalar):
            scalar.wait_ge(angle_ready, 1)
            nc.scalar.activation(sin, rope_at[4], ACT.Sin).then_inc(sin_ready, 1)
            nc.scalar.activation(cos, rope_at[5], ACT.Sin).then_inc(sin_ready, 1)
            norm_scalar_sums(0, mem, lambda e, t: e.wait_ge(mem_landed, 16))
            norm_scalar_sums(1, x, lambda e, t: e.wait_ge(x_landed, 16))
            round_block(0)
            norm_scalar_round(0)
            round_block(1)
            round_block(2)

            def project_out(p):
                scalar.wait_ge(block_used, first["kv"] + p + 1)
                to = PROJ_TO[p]
                n = to.shape[2]
                nc.scalar.copy(to, ps[:, 4 + p % 4, :].rearrange("p (a b) -> p a b", a=2)[:, :, 0:n]).then_inc(proj_out, 1)

            for p in range(11):
                project_out(p)
                round_block(p + 3)
                if p == 1:
                    norm_scalar_round(1)
                if p == 1:
                    scalar.wait_ge(table_landed, 80)
                    nc.scalar.copy(table_hi, table).then_inc(table_hi_ready, 1)
                if p >= 3:
                    bias_scalar(p - 3)
                if p == 7:
                    scalar.wait_ge(gelu_in, 1)
                    nc.scalar.activation(g1, g1, ACT.Tanh, scale=0.7978845608028654).then_inc(gelu_tanh, 1)
            scalar.wait_ge(gate_in, 1)
            act_then(nc.scalar.activation(ge, gaz, ACT.Exp))
            nc.scalar.activation(ge, ge, ACT.Ln, bias=1.0).then_inc(gate_log, 1)
            scalar.wait_ge(ws_psum, 1)
            nc.scalar.copy(ws_t[:, 0:4, :], ps[:, 0, :].rearrange("p (g t) -> p g t", g=4)).then_inc(ws_t_ready, 1)
            nc.scalar.copy(ws_t[:, 4:6, :], ps[:, 1, 0:256].rearrange("p (g t) -> p g t", g=2)).then_inc(ws_t_ready, 1)
            nc.scalar.copy(bs_t, ps[:, 1, 256:262]).then_inc(ws_t_ready, 1)
            scalar.wait_ge(ct_psum, 1)
            nc.scalar.activation(nct, ps[0:6, 2, 0:256], ACT.Copy, scale=-8.0).then_inc(nct_ready, 1)

            def gated_round(n):
                if n == 4:
                    scalar.wait_ge(oa_psum, 1)
                    nc.scalar.copy(h_hi[:, 0:2, :], ps[:, 6, :].rearrange("p (k t) -> p k t", k=2)).then_inc(oa_hi, 1)
                    nc.scalar.copy(h_hi[:, 2, :], ps[:, 7, 0:256]).then_inc(oa_hi, 1)

            attention_scalar(heads_m1, gated_round)
            for b in range(first["out"], first["out"] + 4):
                round_block(b + 3)
            scalar.wait_ge(canvas_written, 64 * CHUNKS)
            add_normed_scalar(0, 0)
            if "F0" in STAGES:
                norm_scalar_sums(2, x, x_after(0))
                norm_scalar_round(2)
                relu_steps(scalar, relu_scalar)
                round_block(first["F0"] + 2 * I0 + 2)
                add_normed_scalar(1, 1)

            def ffn_scalar(st, n, r):
                norm_scalar_sums(n, x, x_after(r - 1))
                norm_scalar_round(n)
                swiglu_steps(scalar, st, swiglu_scalar)
                round_block(first[st] + 3 * I1 + 2)

            if "F1" in STAGES:
                ffn_scalar("F1", 3, 2)
            if "MA" in STAGES:
                norm_scalar_sums(4, x, x_after(2))
                norm_scalar_round(4)

                def turned_a(p):
                    scalar.wait_ge(a_turned, p + 1)
                    if p == 0:
                        scalar.wait_ge(a_small, 80)
                        scalar.wait_ge(q_col_ready, 1)
                    to = qt_a[:, 2 * p:2 * p + 2, :] if p < 4 else kt_a[:, :, :]
                    nc.scalar.activation(to, ps[:, p % 2, :].rearrange("p (k t) -> p k t", k=2), ACT.Copy,
                                         scale=q_col if p < 4 else k_col).then_inc(a_turned_out, 1)

                for p in range(5):
                    b = first["a_in"] + p
                    scalar.wait_ge(block_used, b + 1)
                    bank = ps[:, 4 + p % 4, :]
                    to = qa[:, :, 256 * p:256 * p + 256] if p < 4 else kva
                    nc.scalar.copy(to, bank.rearrange("p (t c) -> p t c", t=TT)).then_inc(a_out_ready, 1)
                    if p >= 2:
                        scalar.wait_ge(a_sums, p - 1)
                    nc.scalar.activation(sq_a[:, p % 2, :], bank, ACT.Square).then_inc(a_squares, 1)
                    round_block(b + 3)
                    if p >= 2:
                        turned_a(p - 2)
                turned_a(3)
                turned_a(4)
                attention_scalar(heads_a)
                for b in range(first["a_out"], first["a_out"] + 4):
                    round_block(b + 3)
            if "F2" in STAGES:
                ffn_scalar("F2", 5, 4)
                ffn_scalar("F3", 6, 5)
            if "MB" in STAGES:
                norm_scalar_sums(7, x, x_after(5))
                norm_scalar_round(7)
                for p in range(2):
                    b = first["b_in"] + p
                    scalar.wait_ge(block_used, b + 1)
                    w = 256 - 96 * p
                    nc.scalar.copy(cb[:, :, 256 * p:256 * p + w],
                                   ps[:, 4 + p, :].rearrange("p (t c) -> p t c", t=TT)[:, :, 0:w]).then_inc(c_out, 1)
                    round_block(b + 3)
                scalar.wait_ge(c_out, 2)
                junk_free()
                for n, cols in enumerate((slice(0, 256), slice(256, 384), slice(384, 416))):
                    for t in range(TT):
                        if n or t:
                            scalar.wait_ge(c_squares, 2 * n + t)
                        nc.scalar.activation(junk[:, cols], cb[:, t, cols], ACT.Square,
                                             accum_out=ss_c[:, 2 * n + t:2 * n + t + 1]).then_inc(c_squares, 1)
                scalar.wait_ge(c_turned, 1)
                nc.scalar.copy(h_hi[:, 0:2, :], ps[:, 0, :].rearrange("p (k t) -> p k t", k=2)).then_inc(c_hi, 1)
                scalar.wait_ge(c_turned, 2)
                nc.scalar.copy(h_hi[:, 2, :], ps[:, 1, 0:TOK]).then_inc(c_hi, 1)
                up = first["b_up"]
                scalar.wait_ge(block_used, up + 1)
                nc.scalar.copy(qb[:, 0, 0:1024], ps[:, 4:6, :].rearrange("p b c -> p (b c)")).then_inc(up_scalar, 1)
                round_block(up + 3)
                scalar.wait_ge(block_used, up + 2)
                nc.scalar.copy(qb[:, :, 1024:1536], ps[:, 2:4, :]).then_inc(up_scalar, 1)
                round_block(up + 4)
                scalar.wait_ge(up_vector, 1)
                scalar.wait_ge(up_scalar, 2)
                for t in range(TT):
                    nc.scalar.activation(scratch[:, t * 1536:(t + 1) * 1536], qb[:, t, :], ACT.Square).then_inc(q_squares, 1)
                scalar.wait_ge(block_used, up + 3)
                nc.scalar.copy(kvb[:, 0, :], ps[:, 4:8, :].rearrange("p b c -> p (b c)")).then_inc(up_scalar, 1)
                round_block(up + 5)
                scalar.wait_ge(q_sums, 1)
                for t in range(TT):
                    if t:
                        scalar.wait_ge(up_vector, 2)
                    else:
                        scalar.wait_ge(up_scalar, 3)
                    nc.scalar.activation(kc[:, t, :, 0:HD], kvb[:, t, :].rearrange("p (h c) -> p h c", h=BH)[:, :, 0:HD],
                                         ACT.Square).then_inc(k_squares, 1)
                scalar.wait_ge(b_small, 64)
                turned_q_scalar(0)
                turned_q_scalar(1)
                attention_scalar(heads_b, lambda n: turned_q_scalar(n + 2))
                for b in range(first["b_out"], first["b_out"] + 4):
                    round_block(b + 3)
            if "F4" in STAGES:
                ffn_scalar("F4", 8, 7)

        @block.vector
        def _(vector):
            vector.wait_ge(pos_landed, 64)
            dve_then(nc.vector.tensor_copy(pos_f, pos_i))
            ang, turns, low, high, sin_in, cos_in = rope_at
            for t in range(TT):
                last = nc.vector.tensor_scalar(ang[:, t, :], freq, pos_f[:, t:t + 1], None, ALU.mult)
            dve_then(last)
            dve_then(nc.vector.tensor_scalar(turns, ang, 0.15915494309189535, 12582912.0, ALU.mult, ALU.add))
            dve_then(nc.vector.tensor_scalar(turns, turns, -12582912.0, None, ALU.add))
            dve_then(nc.vector.scalar_tensor_tensor(low, turns, -6.28125, ang, ALU.mult, ALU.add))
            dve_then(nc.vector.scalar_tensor_tensor(low, turns, -0.0019353071795864769, low, ALU.mult, ALU.add))
            dve_then(nc.vector.tensor_scalar(high, low, 1.5707963267948966, -6.283185307179586, ALU.is_gt, ALU.mult))
            dve_then(nc.vector.scalar_tensor_tensor(high, low, 1.5707963267948966, high, ALU.add, ALU.add))
            nc.vector.tensor_scalar(sin_in, low, 3.1415925, -3.1415925, ALU.min, ALU.max)
            nc.vector.tensor_scalar(cos_in, high, 3.1415925, -3.1415925, ALU.min, ALU.max).then_inc(angle_ready, 1)
            norm_vector_scale(0, 0, mem)
            split_block(0)
            norm_vector_split(0)
            split_block(1)
            split_block(2)
            norm_vector_scale(1, 1, x)

            def gelu(part):
                both = uv[:, :, :].rearrange("p t c -> p (t c)")
                v = uv[:, :, 384:768]
                if part == 0:
                    vector.wait_ge(proj_out, 5)
                    dve_then(nc.vector.tensor_tensor(g1, both, both, ALU.mult))
                    dve_then(nc.vector.tensor_scalar(g1, g1, 0.044715, 1.0, ALU.mult, ALU.add))
                    nc.vector.tensor_tensor(g1, g1, both, ALU.mult).then_inc(gelu_in, 1)
                if part == 1:
                    vector.wait_ge(gelu_tanh, 1)
                    dve_then(nc.vector.scalar_tensor_tensor(both, g1, 1.0, both, ALU.add, ALU.mult))
                    dve_then(nc.vector.tensor_scalar(both, both, 0.5, None, ALU.mult))
                if part == 2:
                    sq = act[:, 0:2, 0:384]
                    dve_then(nc.vector.tensor_tensor(sq, v, v, ALU.mult))
                    for t in range(TT):
                        last = nc.vector.tensor_reduce(ssv[:, t * G:(t + 1) * G], sq[:, t, :].rearrange("p (g d) -> p g d", g=G), AX.X, ALU.add)
                    last.then_inc(v_sumsq, 1)
                    vector.wait_ge(v_rstd, 1)
                    for t in range(TT):
                        last = nc.vector.tensor_tensor(v[:, t, :].rearrange("p (g d) -> p g d", g=G), v[:, t, :].rearrange("p (g d) -> p g d", g=G),
                                                       rsv[:, t * G:(t + 1) * G].to_broadcast([P, G, HD]), ALU.mult)
                    dve_then(last)
                    vector.wait_ge(vgain_landed, 16)
                    for t in range(TT):
                        last = nc.vector.tensor_tensor(v[:, t, :], v[:, t, :], vgain, ALU.mult)
                    last.then_inc(v_ready, 1)

            for p in range(11):
                split_block(p + 3)
                if p == 1:
                    norm_vector_split(1)
                    vector.wait_ge(table_hi_ready, 1)
                    nc.vector.tensor_tensor(table_lo, table, table_hi.bitcast(F32), ALU.subtract).then_inc(table_ready, 1)
                    vector.wait_ge(sin_ready, 2)
                    for name, (g, at, by) in {"q1c": (gq, 0, cos), "q2s": (gq, 16, sin), "q2c": (gq, 16, cos), "q1s": (gq, 0, sin),
                                              "k1c": (gk, 0, cos), "k2s": (gk, 16, sin), "k2c": (gk, 16, cos), "k1s": (gk, 0, sin)}.items():
                        last = nc.vector.tensor_tensor(rot[name], by, g[:, HD + at:HD + at + 16].unsqueeze(1).to_broadcast([P, TT, 16]), ALU.mult)
                    last.then_inc(rot_ready, 1)
                if 1 <= p < 1 + CHUNKS:
                    hot_vector(p - 1)
                if p == 5:
                    gelu(0)
                if p == 8:
                    gelu(1)
                if p == 9:
                    gelu(2)
            vector.wait_ge(bf_landed, 16)
            vector.wait_ge(proj_out, 10)
            for t in range(TT):
                last = nc.vector.tensor_tensor(gz[:, t, :], fv[:, t, 384:390], bf, ALU.add)
            dve_then(last)
            nc.vector.tensor_scalar(gmin, gz, 0.0, None, ALU.min)
            nc.vector.scalar_tensor_tensor(gaz, gz, -1.0, gz, ALU.mult, ALU.min).then_inc(gate_in, 1)
            vector.wait_ge(gate_log, 1)
            nc.vector.tensor_tensor(lf, gmin, ge, ALU.subtract).then_inc(lf_ready, 1)
            vector.wait_ge(mixed_psum, 1)
            for t in range(TT):
                for g in range(G):
                    c = slice(g * HD, (g + 1) * HD)
                    last = nc.vector.scalar_tensor_tensor(oa[:, t, c], ps[:, 6 + t, c], bs_t[:, g:g + 1], uv[:, t, c], ALU.add, ALU.mult)
            last.then_inc(oa_ready, 1)

            def gated_split(n):
                if n == 4:
                    for a, (h, bank) in enumerate(((slice(0, 2), ps[:, 6, :]), (slice(2, 3), ps[:, 7, 0:256]))):
                        vector.wait_ge(oa_hi, a + 1)
                        nc.vector.tensor_tensor(h_lo[:, h, :], bank.rearrange("p (k t) -> p k t", t=TOK), h_hi[:, h, :].bitcast(F32),
                                                ALU.subtract).then_inc(oa_lo, 1)

            attention_vector(heads_m1, gated_split)
            for b in range(first["out"], first["out"] + 4):
                split_block(b + 3)
            add_normed_vector(0, 0, 2)
            if "F0" in STAGES:
                norm_vector_scale(2, 3, x)
                norm_vector_split(2)
                relu_steps(vector, relu_vector)
                split_block(first["F0"] + 2 * I0 + 2)
                add_normed_vector(1, 1, 4)

            def ffn_vector(st, n, g, r):
                norm_vector_scale(n, g, x)
                norm_vector_split(n)
                swiglu_steps(vector, st, swiglu_vector)
                split_block(first[st] + 3 * I1 + 2)
                add_scaled(r, 0.5)

            if "F1" in STAGES:
                ffn_vector("F1", 3, 5, 2)
            if "MA" in STAGES:
                norm_vector_scale(4, 6, x)
                norm_vector_split(4)
                vector.wait_ge(a_small, 80)
                nc.vector.tensor_scalar(q_col, q_col, 0.125, None, ALU.mult).then_inc(q_col_ready, 1)

                def scale_heads(p):
                    vector.wait_ge(a_rstd, p + 1)
                    for t in range(TT):
                        rs = rs_a[:, 8 * p + 4 * t:8 * p + 4 * t + 4]
                        if p < 4:
                            v = qa[:, t, 256 * p:256 * p + 256].rearrange("p (h d) -> p h d", h=4)
                            last = nc.vector.tensor_tensor(v, v, rs.unsqueeze(2).to_broadcast([P, 4, HD]), ALU.mult)
                        else:
                            for twin in range(2):
                                last = nc.vector.tensor_tensor(kd[:, t, :].rearrange("p (g w d) -> p g w d", g=2, w=2)[:, :, twin, :],
                                                               kva[:, t, 0:P].rearrange("p (g d) -> p g d", g=2),
                                                               rs[:, 0:2].unsqueeze(2).to_broadcast([P, 2, HD]), ALU.mult)
                    last.then_inc(a_scaled, 1)

                for p in range(5):
                    vector.wait_ge(a_squares, p + 1)
                    nc.vector.tensor_reduce(ss_a[:, 8 * p:8 * p + 8], sq_a[:, p % 2, :].rearrange("p (h d) -> p h d", h=8),
                                            AX.X, ALU.add).then_inc(a_sums, 1)
                    split_block(first["a_in"] + p + 3)
                    if p:
                        scale_heads(p - 1)
                scale_heads(4)
                attention_vector(heads_a)
                for b in range(first["a_out"], first["a_out"] + 4):
                    split_block(b + 3)
                add_scaled(3, 1.0)
            if "F2" in STAGES:
                ffn_vector("F2", 5, 7, 4)
                ffn_vector("F3", 6, 8, 5)
            if "MB" in STAGES:
                norm_vector_scale(7, 9, x)
                norm_vector_split(7)
                split_block(first["b_in"] + 3)
                split_block(first["b_in"] + 4)
                vector.wait_ge(c_rstd, 2)
                vector.wait_ge(b_small, 64)
                for n, cols in enumerate((slice(0, 256), slice(256, 384))):
                    for t in range(TT):
                        last = nc.vector.scalar_tensor_tensor(cn[:, t, cols], cb[:, t, cols], rs_c[:, 2 * n + t:2 * n + t + 1],
                                                              c_gain[:, cols], ALU.mult, ALU.mult)
                last.then_inc(cn_ready, 1)
                for n, (h, bank) in enumerate(((slice(0, 2), ps[:, 0, :]), (slice(2, 3), ps[:, 1, 0:TOK]))):
                    vector.wait_ge(c_hi, n + 1)
                    nc.vector.tensor_tensor(h_lo[:, h, :], bank.rearrange("p (k t) -> p k t", t=TOK), h_hi[:, h, :].bitcast(F32),
                                            ALU.subtract).then_inc(c_lo, 1)
                kr = [cb[:, :, 384 + 16 * n:400 + 16 * n] for n in range(2)]
                ks = [act[:, 1, 320 + 32 * n:352 + 32 * n].rearrange("p (t c) -> p t c", t=TT) for n in range(2)]
                up = first["b_up"]
                vector.wait_ge(block_used, up + 1)
                nc.vector.tensor_copy(qb[:, 1, 0:1024], ps[:, 6:8, :].rearrange("p b c -> p (b c)")).then_inc(up_vector, 1)
                split_block(up + 3)
                split_block(up + 4)
                dve_then(nc.vector.tensor_tensor(ks[0], kr[0], rot["k1s"], ALU.mult))
                dve_then(nc.vector.tensor_tensor(ks[1], kr[1], rot["k2s"], ALU.mult))
                dve_then(nc.vector.tensor_tensor(kr[0], kr[0], rot["k1c"], ALU.mult))
                dve_then(nc.vector.tensor_tensor(kr[1], kr[1], rot["k2c"], ALU.mult))
                nc.vector.tensor_tensor(kr[0], kr[0], ks[1], ALU.subtract)
                dve_then(nc.vector.tensor_tensor(kr[1], kr[1], ks[0], ALU.add))
                vector.wait_ge(q_squares, 2)
                nc.vector.tensor_reduce(ss_q, scratch[:, :].rearrange("p (h d) -> p h d", d=QK), AX.X, ALU.add).then_inc(q_sums, 1)
                vector.wait_ge(block_used, up + 3)
                nc.vector.tensor_copy(kvb[:, 1, :], ps[:, 0:4, :].rearrange("p b c -> p (b c)")).then_inc(up_vector, 1)
                split_block(up + 5)
                vector.wait_ge(k_squares, 2)
                for t in range(TT):
                    last = nc.vector.tensor_reduce(ss_k[:, t * BH:(t + 1) * BH], kc[:, t, :, 0:HD], AX.X, ALU.add)
                dve_then(last)
                for t in range(TT):
                    last = nc.vector.tensor_scalar(ss_k[:, t * BH:(t + 1) * BH], ss_k[:, t * BH:(t + 1) * BH], ss_c[:, 4 + t:5 + t], None, ALU.add)
                last.then_inc(k_sums, 1)
                vector.wait_ge(qk_rstd, 2)
                for t in range(TT):
                    rs = rs_k[:, t * BH:(t + 1) * BH].unsqueeze(2)
                    nc.vector.tensor_tensor(kc[:, t, :, 0:HD], kvb[:, t, :].rearrange("p (h c) -> p h c", h=BH)[:, :, 0:HD],
                                            rs.to_broadcast([P, BH, HD]), ALU.mult)
                    last = nc.vector.tensor_tensor(kc[:, t, :, HD:QK], cb[:, t, 384:416].unsqueeze(1).to_broadcast([P, BH, 32]),
                                                   rs.to_broadcast([P, BH, 32]), ALU.mult)
                last.then_inc(kc_ready, 1)
                turned_k_vector(0)
                turned_k_vector(1)
                attention_vector(heads_b, lambda n: turned_k_vector(n + 2))
                for b in range(first["b_out"], first["b_out"] + 4):
                    split_block(b + 3)
                add_scaled(6, 1.0)
            if "F4" in STAGES:
                ffn_vector("F4", 8, 10, 7)

        @block.tensor
        def _(tensor):
            tensor.wait_ge(tables_ready, 1)
            norm_tensor_turn(0)

            def project(p):
                if p >= 4:
                    tensor.wait_ge(proj_out, p - 3)
                b = first["kv"] + p
                wait_h = {0: 0, 2: 4}.get(p)
                if p in PROJ_FEATURES:
                    features_out(b, lambda f: ps[:, 4 + p % 4, f * TOK:(f + 1) * TOK], wait_h=wait_h)
                else:
                    tokens_out(b, lambda t, c, w: ps[:, 4 + p % 4, t * TOK + c:t * TOK + c + w], wait_h=wait_h)

            project(0)
            project(1)
            norm_tensor_turn(1)
            for p in range(2, 11):
                project(p)
                if p == 2:
                    tensor.wait_ge(table_ready, 1)
                if p < 2 + CHUNKS:
                    bias_tensor(p - 2)
            tensor.wait_ge(ws_ready, 1)
            tensor.wait_ge(bias_out, CHUNKS)
            for g in range(G):
                nc.tensor.transpose(ps[:, g // 4, g % 4 * P:(g % 4 + 1) * P], ws[:, g, :], ident[:, :])
            nc.tensor.transpose(ps[:, 1, 256:262], bs, ident[0:6, 0:6]).then_inc(ws_psum, 1)
            tensor.wait_ge(lf_ready, 1)
            nc.tensor.matmul(ps[0:6, 2, 0:TOK], lf[:, 0, :], tri[:, P:3 * P], start=True, stop=False, skip_group_check=True)
            nc.tensor.matmul(ps[0:6, 2, 0:TOK], lf[:, 1, :], tri[:, 0:2 * P], start=False, stop=True, skip_group_check=True).then_inc(ct_psum, 1)
            tensor.wait_ge(ws_t_ready, 3)
            tensor.wait_ge(v_ready, 1)
            tensor.wait_ge(proj_out, 11)
            for t in range(TT):
                for g in range(G):
                    last = nc.tensor.matmul(ps[:, 6 + t, g * HD:(g + 1) * HD], ws_t[:, g, :], uv[:, t, 384 + g * HD:384 + (g + 1) * HD],
                                            start=True, stop=True, skip_group_check=True)
            last.then_inc(mixed_psum, 1)
            tensor.wait_ge(nct_ready, 1)
            tensor.wait_ge(tables_ready, 2)

            def gated_turn(n):
                if n == 3:
                    tensor.wait_ge(oa_ready, 1)
                    for k in range(3):
                        for t in range(TT):
                            last = nc.tensor.transpose(ps[:, 6 + k // 2, k % 2 * TOK + t * P:k % 2 * TOK + (t + 1) * P],
                                                       oa[:, t, k * P:(k + 1) * P], ident[:, :])
                    last.then_inc(oa_psum, 1)

            attention_tensor(heads_m1, gated_turn)

            def output_projection(stage, pairs):
                tensor.wait_ge(o_lo_ready, pairs)
                for c in range(4):
                    tokens_out(first[stage] + c, lambda t, c0, w: y_bank(t, 256 * c + c0, w))

            tensor.wait_ge(oa_lo, 2)
            output_projection("out", 5)
            if "F0" in STAGES:
                norm_tensor_turn(2)
                relu_steps(tensor, relu_tensor)
                second_product("F0", b_down(I0 - 1), I0 - 1, (I0 - 1) % 3, False, True)

            def ffn_tensor(st, n):
                norm_tensor_turn(n)
                swiglu_steps(tensor, st, lambda st, s, turn=0: swiglu_tensor(st, n, s, turn))
                second_product(st, b_lower(st, I1 - 1), I1 - 1, (I1 - 1) % 2, False, True)

            if "F1" in STAGES:
                ffn_tensor("F1", 3)
            if "MA" in STAGES:
                norm_tensor_turn(4)

                def turn_a(p):
                    tensor.wait_ge(a_scaled, p + 1)
                    if p >= 2:
                        tensor.wait_ge(a_turned_out, p - 1)
                    for k in range(2):
                        for t in range(TT):
                            c = k * P
                            source = qa[:, t, 256 * p + c:256 * p + c + P] if p < 4 else kd[:, t, c:c + P]
                            last = nc.tensor.transpose(ps[:, p % 2, k * TOK + t * P:k * TOK + (t + 1) * P], source, ident[:, :])
                    last.then_inc(a_turned, 1)

                for p in range(5):
                    if p >= 4:
                        tensor.wait_ge(a_squares, p - 3)
                    tokens_out(first["a_in"] + p, lambda t, c, w: ps[:, 4 + p % 4, t * TOK + c:t * TOK + c + w],
                               wait_h=16 if p == 0 else None)
                    if p >= 2:
                        turn_a(p - 2)
                turn_a(3)
                turn_a(4)
                tensor.wait_ge(a_turned_out, 5)
                attention_tensor(heads_a)
                output_projection("a_out", 13)
            if "F2" in STAGES:
                ffn_tensor("F2", 5)
                ffn_tensor("F3", 6)
            if "MB" in STAGES:
                norm_tensor_turn(7)
                for p in range(2):
                    tokens_out(first["b_in"] + p, lambda t, c, w: ps[:, 4 + p, t * TOK + c:t * TOK + c + w],
                               wait_h=28 if p == 0 else None)
                tensor.wait_ge(cn_ready, 1)
                for k in range(3):
                    for t in range(TT):
                        last = nc.tensor.transpose(ps[:, k // 2, k % 2 * TOK + t * P:k % 2 * TOK + (t + 1) * P],
                                                   cn[:, t, k * P:(k + 1) * P], ident[:, :])
                    if k:
                        last.then_inc(c_turned, 1)
                tensor.wait_ge(c_lo, 2)
                up = first["b_up"]
                tokens_out(up, y_bank)
                tokens_out(up + 1, lambda t, c, w: ps[:, 2 + t, 0:w])
                tensor.wait_ge(up_scalar, 2)
                tensor.wait_ge(up_vector, 1)
                tokens_out(up + 2, lambda t, c, w: ps[:, (4 if t == 0 else 0) + c // 512, 0:w], h0=2)
                tensor.wait_ge(up_scalar, 3)
                tensor.wait_ge(up_vector, 2)
                tensor.wait_ge(q_roped, 1)
                tensor.wait_ge(kc_ready, 1)
                turn_qk_tensor(0)
                turn_qk_tensor(1)
                attention_tensor(heads_b, lambda n: turn_qk_tensor(n + 2))
                output_projection("b_out", 21)
            if "F4" in STAGES:
                ffn_tensor("F4", 8)


def kernel(**inputs):
    import numpy as np
    import concourse.bacc as bacc
    from concourse.bass_utils import run_bass_kernel_spmd

    nc = bacc.Bacc("TRN2", target_bir_lowering=False, num_devices=1)
    arrays, args = {}, {}
    for name, value in inputs.items():
        a = np.ascontiguousarray(value)
        arrays[f"in_{name}"] = a
        args[name] = nc.dram_tensor(f"in_{name}", a.shape, mybir.dt.from_np(a.dtype), kind="ExternalInput").ap()
    first_of = [-3.0e38] + [float(k if k <= 16 else math.ceil(16 * 8 ** ((k - 16) / 16))) for k in range(1, 32)]
    pairs = np.array([[a, b] for a, b in zip(first_of, first_of[1:] + [3.0e38])], np.float32)
    constants = {"bucket_edges": np.concatenate([pairs] * 4),
                 "rope_freq": (np.float32(10000.0) ** (-np.arange(0, 32, 2, dtype=np.float32) / np.float32(32)))[None, :]}
    for name, a in constants.items():
        arrays[f"const_{name}"] = a
        args[name] = nc.dram_tensor(f"const_{name}", a.shape, F32, kind="ExternalInput").ap()
    out = nc.dram_tensor("out", (TOK, D), F32, kind="ExternalOutput").ap()
    build(nc, args, out)
    r = run_bass_kernel_spmd(nc, [arrays], core_ids=[0])
    return r.results[0]["out"].reshape(1, TOK, D)
```

```python
import math
from contextlib import ExitStack

import concourse.bass as bass
from concourse import mybir

F32 = mybir.dt.float32
F32R = mybir.dt.float32r
I32 = mybir.dt.int32
ALU = mybir.AluOpType
ACT = mybir.ActivationFunctionType
AX = mybir.AxisListType

P = 128
TT = 2
TOK = TT * P
D = 1024
KD = D // P
HD = 64
EPS = 1e-6
NEG = -1e30

RAW = 6
RING = 3
BLK = 2048

STAGES = ["M1", "F0", "F1", "MA", "F2", "F3", "MB", "F4"]


def build(nc, i, out):
    blocks = []
    first = {}

    def columns(w, c, n):
        return w[:, c:c + n].rearrange("(k p) n -> p k n", p=P)

    FF0, FF = 4096, 2816
    I0, I1 = FF0 // 256, FF // 256
    first["kv"] = len(blocks)
    blocks += [columns(i["w_mem_kv"][0], c, 256) for c in (0, 256)]
    first["in"] = len(blocks)
    w_in_cuts = [(0, 256), (256, 256), (512, 256), (768, 256), (1024, 256), (1280, 256),
                 (1536, 256), (1792, 134), (1926, 256)]
    blocks += [columns(i["w_in"][0], c, n) for c, n in w_in_cuts]
    first["out"] = len(blocks)
    blocks += [columns(i["w_out"][0], c, 256) for c in range(0, D, 256)]
    first["F0"] = len(blocks)
    for s in range(I0 + 1 if "F0" in STAGES else 0):
        if s < I0:
            blocks.append(columns(i["w_ff1"][0], 256 * s, 256))
        if s:
            blocks.append(i["w_ff2"][0][256 * (s - 1):256 * s, :].rearrange("(k p) n -> p k n", p=P))
    swiglu = {"F1": ("ffn1", 0), "F2": ("ffn2", 0), "F3": ("ffn1", 1), "F4": ("ffn2", 1)}

    def swiglu_weights(stage):
        name, layer = swiglu[stage]
        return [i[f"{name}_w{x}_2"][layer] for x in "gud"]

    def swiglu_blocks(stage):
        wg, wu, wd = swiglu_weights(stage)
        first[stage] = len(blocks)
        for s in range(I1 + 1):
            if s < I1:
                blocks.append(columns(wg, 256 * s, 256))
                blocks.append(columns(wu, 256 * s, 256))
            if s:
                blocks.append(wd[256 * (s - 1):256 * s, :].rearrange("(k p) n -> p k n", p=P))

    if "F1" in STAGES:
        swiglu_blocks("F1")
    if "MA" in STAGES:
        first["a_in"] = len(blocks)
        blocks += [columns(i["a_w_in_2"][0], c, 256) for c in (1024, 0, 256, 512, 768)]
        first["a_out"] = len(blocks)
        blocks += [columns(i["a_w_out_2"][0], c, 256) for c in range(0, D, 256)]
    if "F2" in STAGES:
        swiglu_blocks("F2")
        swiglu_blocks("F3")
    if "MB" in STAGES:
        first["b_in"] = len(blocks)
        blocks += [columns(i["b_w_in_2"][0], c, n) for c, n in ((256, 160), (0, 256))]
        first["b_up"] = len(blocks)
        blocks += [columns(i["b_w_ukv_2"][0], 0, 2048)]
        blocks += [columns(i["b_w_uq_2"][0], c, n) for c, n in ((0, 1024), (1024, 512))]
        first["b_out"] = len(blocks)
        blocks += [columns(i["b_w_out_2"][0], c, 256) for c in range(0, D, 256)]
    if "F4" in STAGES:
        swiglu_blocks("F4")
    NB = len(blocks)

    gain_sources = [i["norm_mem"], i["norm_pre_mix"], i["norm_pre_ffn"], i["ffn_norm1_2"], i["mix_norm_2"], i["ffn_norm2_2"]]
    GAIN_ROWS = 9 * KD
    gain_at = [KD * place for place in (0, 1, 2, 3, 5, 7, 4, 6, 8)]

    with ExitStack() as ctx:
        def sb(name, shape, dt=F32):
            return ctx.enter_context(nc.sbuf_tensor(name, shape, dt))

        def sem(name):
            return ctx.enter_context(nc.semaphore(name))

        raw = sb("raw", [P, RAW, BLK])
        w_hi = sb("w_hi", [P, RING, BLK], F32R)
        w_lo = sb("w_lo", [P, RING, BLK], F32R)
        x = sb("x", [P, TT, D])
        h_hi = sb("h_hi", [P, KD, TOK], F32R)
        h_lo = sb("h_lo", [P, KD, TOK], F32R)
        scratch = sb("scratch", [P, 3 * D])
        xn = scratch[:, 0:2 * D].rearrange("p (t d) -> p t d", t=TT)
        junk = scratch[:, 2 * D:3 * D]
        act = sb("act", [P, 3, 512])
        act_hi = sb("act_hi", [P, 3, 512], F32R)
        act_lo = sb("act_lo", [P, 3, 512], F32R)
        post_gain = sb("post_gain", [P, D])
        gain_rows = scratch[0:GAIN_ROWS, 0:P]
        gain_col = sb("gain_col", [P, GAIN_ROWS])
        diag = sb("diag", [P, TT, P])
        arena = sb("arena", [P, 10700])
        ident = sb("ident", [P, P])
        tri = sb("tri", [P, 3 * P])
        causal = sb("causal", [P, 3 * P])
        sums = sb("sums", [P, 64])
        rstd = sb("rstd", [P, 64])
        small = sb("small", [P, 256])
        keep = sb("keep", [P, 544])
        halves = sb("halves", [P, 36])
        ps = ctx.enter_context(nc.psum_tensor("ps", [P, 8, 512], F32))

        landed = [sem(f"landed{s}") for s in range(RAW)]
        hi_ready = sem("hi_ready")
        lo_ready = sem("lo_ready")
        block_used = sem("block_used")
        post_gain_landed = sem("post_gain_landed")
        gain_landed = sem("gain_landed")
        gain_psum = sem("gain_psum")
        gain_ready = sem("gain_ready")
        mem_landed = [sem(f"mem_landed{t}") for t in range(TT)]
        x_landed = sem("x_landed")
        tables_ready = sem("tables_ready")
        dve_step = sem("dve_step")
        act_step = sem("act_step")
        pool_step = sem("pool_step")
        sumsq_ready = sem("sumsq_ready")
        diag_ready = sem("diag_ready")
        h_psum = sem("h_psum")
        h_hi_ready = sem("h_hi_ready")
        h_lo_ready = sem("h_lo_ready")
        y_sumsq = sem("y_sumsq")
        norm_rstd = sem("norm_rstd")
        y_rstd = sem("y_rstd")
        v_sumsq = sem("v_sumsq")
        v_rstd = sem("v_rstd")
        x_ready = sem("x_ready")
        y_tile = sem("y_tile")
        out_landed = sem("out_landed")

        chain = {"dve": 0, "act": 0, "pool": 0}

        def dve_then(instruction):
            chain["dve"] += 1
            instruction.then_inc(dve_step, 1)
            nc.vector.wait_ge(dve_step, chain["dve"])

        def act_then(instruction):
            chain["act"] += 1
            instruction.then_inc(act_step, 1)
            nc.scalar.wait_ge(act_step, chain["act"])

        def pool_then(instruction):
            chain["pool"] += 1
            instruction.then_inc(pool_step, 1)
            nc.gpsimd.wait_ge(pool_step, chain["pool"])

        def view(ring, slot, b_shape):
            k, n = b_shape
            return ring[:, slot, 0:k * n].rearrange("p (k n) -> p k n", k=k)

        def shape(b):
            return blocks[b].shape[1], blocks[b].shape[2]

        def parts(b):
            return view(w_hi, b % RING, shape(b)), view(w_lo, b % RING, shape(b))

        def load(b, source=None, turn=0):
            if b >= RAW:
                nc.sync.wait_ge(lo_ready, b - RAW + 1 + RAW * turn)
            source = blocks[b] if source is None else source
            nc.sync.dma_start(view(raw, b % RAW, shape(b)), source).then_inc(landed[b % RAW], 16)
            if 0 <= b - STORE_LAG < CHUNKS:
                bias_store(b - STORE_LAG)

        def size(b):
            k, n = shape(b)
            return k * n

        def round_block(b, turn=0):
            if b >= NB:
                return
            if b >= RING:
                nc.scalar.wait_ge(block_used, b - RING + 1 + RAW * turn)
            nc.scalar.wait_ge(landed[b % RAW], 16 * (b // RAW + 1) + 16 * turn)
            n = size(b)
            nc.scalar.copy(w_hi[:, b % RING, 0:n], raw[:, b % RAW, 0:n]).then_inc(hi_ready, 1)

        def split_block(b, turn=0):
            if b >= NB:
                return
            nc.vector.wait_ge(hi_ready, b + 1 + RAW * turn)
            n = size(b)
            nc.vector.tensor_tensor(w_lo[:, b % RING, 0:n], raw[:, b % RAW, 0:n],
                                    w_hi[:, b % RING, 0:n].bitcast(F32), ALU.subtract).then_inc(lo_ready, 1)

        QUARTERS = 4

        def split_quarter(b, quarter):
            if quarter == 0:
                nc.vector.wait_ge(hi_ready, b + 1)
            n = size(b) // QUARTERS
            cols = slice(quarter * n, (quarter + 1) * n)
            last = nc.vector.tensor_tensor(w_lo[:, b % RING, cols], raw[:, b % RAW, cols],
                                           w_hi[:, b % RING, cols].bitcast(F32), ALU.subtract)
            if quarter == QUARTERS - 1:
                last.then_inc(lo_ready, 1)

        def product(to, still, moving, start, stop):
            nc.tensor.matmul(to, still[0], moving[0], start=start, stop=False, skip_group_check=True)
            nc.tensor.matmul(to, still[0], moving[1], start=False, stop=False, skip_group_check=True)
            return nc.tensor.matmul(to, still[1], moving[0], start=False, stop=stop, skip_group_check=True)

        def features_out(b, to, kn=KD, turn=0, wait_h=None):
            nc.tensor.wait_ge(lo_ready, b + 1 + RAW * turn)
            hi, lo = parts(b)
            k_n, cols = shape(b)
            for f in range(cols // P):
                for k in range(k_n):
                    if wait_h is not None and f == 0 and k % 2 == 0:
                        nc.tensor.wait_ge(h_lo_ready, wait_h + k // 2 + 1)
                    last = product(to(f), (hi[:, k, f * P:(f + 1) * P], lo[:, k, f * P:(f + 1) * P]),
                                   (h_hi[:, k, :], h_lo[:, k, :]), k == 0, k == k_n - 1)
            last.then_inc(block_used, 1)

        def tokens_out(b, to, turn=0, wait_h=None, h0=0, wait_k=None, half_done=None, before=None):
            nc.tensor.wait_ge(lo_ready, b + 1 + RAW * turn)
            hi, lo = parts(b)
            k_n, cols = shape(b)
            order = (1, 0) if wait_k is not None else (0, 1)
            for t in order:
                if before and t == order[1]:
                    before()
                for c in range(0, cols, 512):
                    w = min(512, cols - c)
                    for k in range(k_n):
                        if wait_h is not None and t == order[0] and c == 0 and k % 2 == 0:
                            nc.tensor.wait_ge(h_lo_ready, wait_h + k // 2 + 1)
                        if wait_k is not None and t == order[0] and c == 0:
                            wait_k(k)
                        last = product(to(t, c, w), (h_hi[:, h0 + k, t * P:(t + 1) * P], h_lo[:, h0 + k, t * P:(t + 1) * P]),
                                       (hi[:, k, c:c + w], lo[:, k, c:c + w]), k == 0, k == k_n - 1)
                if half_done and t == 0:
                    last.then_inc(half_done, 1)
            last.then_inc(block_used, 1)

        def y_bank(t, c, w):
            return ps[:, 4 + 2 * t + c // 512, c % 512:c % 512 + w]

        squares = {"h": 0, "y": 0}

        def junk_free():
            if squares["h"]:
                nc.scalar.wait_ge(sumsq_ready, squares["h"])
            if squares["y"]:
                nc.scalar.wait_ge(y_sumsq, squares["y"])

        def norm_scalar_sums(n, source, ready):
            for t in range(TT):
                ready(nc.scalar, t)
                junk_free()
                squares["h"] += 1
                nc.scalar.activation(junk, source[:, t, :], ACT.Square,
                                     accum_out=sums[:, 2 * n + t:2 * n + t + 1]).then_inc(sumsq_ready, 1)

        def rsqrt_pool(to, sums_of, count, done, eps=EPS, negate=False):
            n = sums_of.shape[1]
            pool_then(nc.gpsimd.tensor_scalar(to, sums_of, 1.0 / count, eps, ALU.mult, ALU.add))
            last = nc.gpsimd.tensor_tensor(to, to, halves[:, 0:n], ALU.pow)
            if negate:
                pool_then(last)
                last = nc.gpsimd.tensor_scalar(to, to, -1.0, None, ALU.mult)
            last.then_inc(done, 1)

        def norm_pool(n):
            for t in range(TT):
                c = 2 * n + t
                nc.gpsimd.wait_ge(sumsq_ready, c + 1)
                rsqrt_pool(rstd[:, c:c + 1], sums[:, c:c + 1], D, norm_rstd)

        def add_normed_pool(m):
            for t in range(TT):
                c = 32 + 2 * m + t
                nc.gpsimd.wait_ge(y_sumsq, 2 * m + t + 1)
                rsqrt_pool(rstd[:, c:c + 1], sums[:, c:c + 1], D, y_rstd)

        def norm_vector_diag(n):
            for t in range(TT):
                c = 2 * n + t
                nc.vector.wait_ge(norm_rstd, c + 1)
                if t == 0:
                    if n:
                        nc.vector.wait_ge(h_psum, 4 * n)
                    else:
                        nc.vector.wait_ge(tables_ready, 1)
                nc.vector.tensor_scalar(diag[:, t, :], ident[:, :], rstd[:, c:c + 1], None, ALU.mult).then_inc(diag_ready, 1)

        def norm_tensor_turn(n, source):
            for t in range(TT):
                nc.tensor.wait_ge(diag_ready, 2 * n + t + 1)
                for k in range(KD):
                    col = (k % 2) * TOK + t * P
                    last = nc.tensor.matmul(ps[:, k // 2, col:col + P], source[:, t, k * P:(k + 1) * P], diag[:, t, :],
                                            start=True, stop=True, skip_group_check=True)
                    if t == TT - 1 and k % 2:
                        last.then_inc(h_psum, 1)

        def norm_gain(n, k):
            return gain_col[:, gain_at[n] + k:gain_at[n] + k + 1]

        def norm_scalar_round(n):
            for j in range(4):
                nc.scalar.wait_ge(h_psum, 4 * n + j + 1)
                for half in range(2):
                    k = 2 * j + half
                    last = nc.scalar.activation(h_hi[:, k, :], ps[:, j, half * TOK:(half + 1) * TOK], ACT.Copy, scale=norm_gain(n, k))
                last.then_inc(h_hi_ready, 1)

        def norm_vector_split(n):
            for j in range(4):
                nc.vector.wait_ge(h_hi_ready, 4 * n + j + 1)
                for half in range(2):
                    k = 2 * j + half
                    last = nc.vector.scalar_tensor_tensor(h_lo[:, k, :], ps[:, j, half * TOK:(half + 1) * TOK], norm_gain(n, k),
                                                          h_hi[:, k, :].bitcast(F32), ALU.mult, ALU.subtract)
                last.then_inc(h_lo_ready, 1)

        def y_block(r):
            return [first["out"] + 3, first["F0"] + 2 * I0 - 1,
                    first.get("F1", 0) + 3 * I1 - 1, first.get("a_out", 0) + 3, first.get("F2", 0) + 3 * I1 - 1,
                    first.get("F3", 0) + 3 * I1 - 1, first.get("b_out", 0) + 3, first.get("F4", 0) + 3 * I1 - 1][r]

        def y_wait(engine, r, t):
            if t == 0:
                engine.wait_ge(y_tile, r + 1)
            else:
                engine.wait_ge(block_used, y_block(r) + 1)

        def add_scaled(r, scale):
            for t in range(TT):
                y_wait(nc.vector, r, t)
                nc.vector.scalar_tensor_tensor(x[:, t, :], ps[:, 4 + 2 * t:6 + 2 * t, :].rearrange("p b c -> p (b c)"), scale,
                                               x[:, t, :], ALU.mult, ALU.add).then_inc(x_ready, 1)

        def add_normed_scalar(r, m):
            for t in range(TT):
                y_wait(nc.scalar, r, t)
                junk_free()
                squares["y"] += 1
                nc.scalar.activation(junk, ps[:, 4 + 2 * t:6 + 2 * t, :].rearrange("p b c -> p (b c)"), ACT.Square,
                                     accum_out=sums[:, 32 + 2 * m + t:33 + 2 * m + t]).then_inc(y_sumsq, 1)

        def add_normed_vector(m):
            nc.vector.wait_ge(post_gain_landed, 16 * (m + 1))
            for t in range(TT):
                nc.vector.wait_ge(y_sumsq, 2 * m + t + 1)
                dve_then(nc.vector.tensor_tensor(xn[:, t, :], ps[:, 4 + 2 * t:6 + 2 * t, :].rearrange("p b c -> p (b c)"),
                                                 post_gain[:, :], ALU.mult))
                c = 32 + 2 * m + t
                nc.vector.wait_ge(y_rstd, 2 * m + t + 1)
                nc.vector.scalar_tensor_tensor(x[:, t, :], xn[:, t, :], rstd[:, c:c + 1], x[:, t, :], ALU.mult, ALU.add).then_inc(x_ready, 1)

        def x_after(r):
            def wait(engine, t):
                engine.wait_ge(x_ready, 2 * r + t + 1)
            return wait

        def carve(at, *dims):
            n = 1
            for d in dims:
                n *= d
            ap = arena[:, at:at + n]
            if len(dims) == 2:
                ap = ap.rearrange("p (a b) -> p a b", a=dims[0])
            elif len(dims) == 3:
                ap = ap.rearrange("p (a b c) -> p a b c", a=dims[0], b=dims[1])
            return ap

        S_AT = 10700 - 2 * 1024
        prob = [arena[:, S_AT:S_AT + 512], arena[:, S_AT + 512:S_AT + 1024], act[:, 2, :]]
        prob_t = carve(S_AT + 1024, 2, 512)
        nmx, den, rden, sink_e = (small[:, 160 + 4 * n:164 + 4 * n].rearrange("p (b t) -> p b t", b=2) for n in range(4))
        scores_psum = sem("scores_psum")
        negmax_ready = sem("negmax_ready")
        exp_ready = sem("exp_ready")
        prob_ready = sem("prob_ready")
        turned_psum = sem("turned_psum")
        turned_ready = sem("turned_ready")
        o_psum = sem("o_psum")
        o_hi_ready = sem("o_hi_ready")
        o_lo_ready = sem("o_lo_ready")

        class Head:

            def __init__(self, e, q, k, v, mask, minus_scale, tile, row, causal=True, extra=None, sink=None, minus_sink=None,
                         wait_tensor=None, wait_vector=None):
                self.e, self.q, self.k, self.v, self.mask, self.minus_scale = e, q, k, v, mask, minus_scale
                self.tile, self.row, self.causal, self.extra, self.sink = tile, row, causal, extra, sink
                self.wait_tensor, self.wait_vector, self.minus_sink = wait_tensor, wait_vector, minus_sink

            def keys(self, t):
                return (t + 1) * P if self.causal else TOK

        def scores_tensor(h):
            e = h.e
            if e >= 2:
                nc.tensor.wait_ge(negmax_ready, e - 1)
            if h.wait_tensor:
                h.wait_tensor()
            for t in range(TT):
                n = h.keys(t)
                to = ps[:, e % 2, t * TOK:t * TOK + n]
                last = nc.tensor.matmul(to, h.q(t), h.k(n), start=True, stop=h.extra is None, skip_group_check=True)
                if h.extra:
                    last = nc.tensor.matmul(to, h.extra[0], h.extra[1](n), start=False, stop=True, skip_group_check=True)
            last.then_inc(scores_psum, 1)

        def turn_tensor(h):
            e = h.e
            nc.tensor.wait_ge(prob_ready, e + 1)
            if e >= 2:
                nc.tensor.wait_ge(turned_ready, e - 1)
            for s in range(TT):
                for t in range(s if h.causal else 0, TT):
                    col = s * TOK + t * P - (s * P if h.causal else 0)
                    last = nc.tensor.transpose(ps[:, 2 + e % 2, col:col + P],
                                               prob[e % 3][:, t * TOK + s * P:t * TOK + (s + 1) * P], ident[:, :])
            last.then_inc(turned_psum, 1)

        def values_tensor(h):
            e = h.e
            pair = e // 2
            nc.tensor.wait_ge(turned_ready, e + 1)
            if e % 2 == 0 and pair >= 2:
                nc.tensor.wait_ge(o_lo_ready, pair - 1)
            q0 = P if h.causal else 0
            to = ps[h.row:h.row + HD, 4 + pair % 2, :]
            nc.tensor.matmul(to[:, 0:TOK], h.v(0), prob_t[:, e % 2, 0:TOK], start=True, stop=False, skip_group_check=True)
            nc.tensor.matmul(to[:, q0:TOK], h.v(1), prob_t[:, e % 2, TOK:2 * TOK - q0], start=False, stop=True,
                             skip_group_check=True).then_inc(o_psum, 1)

        def attention_tensor(heads, between=None):
            for n in range(len(heads) + 3):
                if n < len(heads):
                    scores_tensor(heads[n])
                if between:
                    between(n)
                if 2 <= n < len(heads) + 2:
                    turn_tensor(heads[n - 2])
                if n >= 3:
                    values_tensor(heads[n - 3])

        def exp_scalar(h):
            e = h.e
            nc.scalar.wait_ge(negmax_ready, e + 1)
            for t in range(TT):
                sc = prob[e % 3][:, t * TOK:t * TOK + h.keys(t)]
                last = nc.scalar.activation(sc, sc, ACT.Exp, scale=-1.0, bias=nmx[:, e % 2, t:t + 1], accum_out=den[:, e % 2, t:t + 1])
            if h.sink is not None:
                last = nc.scalar.activation(sink_e[:, e % 2, :], nmx[:, e % 2, :], ACT.Exp, bias=h.sink)
            last.then_inc(exp_ready, 1)

        def turned_scalar(h):
            e = h.e
            nc.scalar.wait_ge(turned_psum, e + 1)
            if e >= 2:
                nc.scalar.wait_ge(o_psum, e - 1)
            n = 3 * P if h.causal else 4 * P
            nc.scalar.copy(prob_t[:, e % 2, 0:n], ps[:, 2 + e % 2, 0:n]).then_inc(turned_ready, 1)

        def out_scalar(h):
            nc.scalar.wait_ge(o_psum, h.e + 1)
            nc.scalar.copy(h_hi[:, h.tile, :], ps[:, 4 + h.e // 2 % 2, 0:TOK]).then_inc(o_hi_ready, 1)

        def attention_scalar(heads, between=None):
            for n in range(len(heads) + 4):
                if between:
                    between(n)
                if 2 <= n < len(heads) + 2:
                    turned_scalar(heads[n - 2])
                if n < len(heads):
                    exp_scalar(heads[n])
                if n >= 4 and n % 2:
                    out_scalar(heads[n - 4])

        def max_vector(h):
            e = h.e
            nc.vector.wait_ge(scores_psum, e + 1)
            if e >= 3:
                nc.vector.wait_ge(turned_psum, e - 2)
            if h.wait_vector:
                h.wait_vector()
            for t in range(TT):
                n = h.keys(t)
                last = nc.vector.tensor_tensor_reduce(prob[e % 3][:, t * TOK:t * TOK + n], ps[:, e % 2, t * TOK:t * TOK + n],
                                                      h.mask(t), h.minus_scale(t), 3.0e38 if h.sink is None else h.minus_sink,
                                                      ALU.add, ALU.min, nmx[:, e % 2, t:t + 1])
            last.then_inc(negmax_ready, 1)

        def prob_vector(h):
            e = h.e
            nc.vector.wait_ge(exp_ready, e + 1)
            if h.sink is not None:
                dve_then(nc.vector.tensor_tensor(den[:, e % 2, :], den[:, e % 2, :], sink_e[:, e % 2, :], ALU.add))
            dve_then(nc.vector.reciprocal(rden[:, e % 2, :], den[:, e % 2, :]))
            for t in range(TT):
                sc = prob[e % 3][:, t * TOK:t * TOK + h.keys(t)]
                last = nc.vector.tensor_scalar(sc, sc, rden[:, e % 2, t:t + 1], None, ALU.mult)
            last.then_inc(prob_ready, 1)

        def out_vector(h):
            pair = h.e // 2
            nc.vector.wait_ge(o_hi_ready, pair + 1)
            nc.vector.tensor_tensor(h_lo[:, h.tile, :], ps[:, 4 + pair % 2, 0:TOK], h_hi[:, h.tile, :].bitcast(F32),
                                    ALU.subtract).then_inc(o_lo_ready, 1)

        def attention_vector(heads, between=None):
            for n in range(len(heads) + 5):
                if between:
                    between(n)
                if n < len(heads):
                    max_vector(heads[n])
                if 1 <= n <= len(heads):
                    prob_vector(heads[n - 1])
                if n >= 6 and n % 2 == 0:
                    out_vector(heads[n - 5])

        G, H1, HM = 6, 6, 4
        mem = carve(0, TT, D)
        uv = carve(0, TT, 768)
        fqk = carve(1536, 6, TOK)
        fv = carve(3072, TT, 390)
        mq = carve(3852, 2, TOK)
        km = carve(4364, 2, TOK)
        vm = carve(4876, TT, 256)
        ws = carve(5388, G, P)
        oa = carve(5388, TT, 384)
        ws_t = carve(6156, G, P)
        sel = arena[0:6, 6924:7692].rearrange("p (h c) -> p h c", h=H1)
        nct = arena[0:6, 7692:7948]
        vgain = carve(7948, 384)
        bs = arena[0:6, 8332:8460]
        ssv, rsv = small[:, 0:12], small[:, 12:24]
        gz, gaz, gmin, ge, lf = (small[:, 24 + 12 * n:36 + 12 * n].rearrange("p (t h) -> p t h", t=TT) for n in range(5))
        bs_t = small[:, 84:90]
        bf = small[:, 90:96]
        g1 = act[:, :, :].rearrange("p a b -> p (a b)")
        small_landed = sem("small_landed")
        bf_landed = sem("bf_landed")
        vgain_landed = sem("vgain_landed")
        ws_ready = sem("ws_ready")
        proj_out = sem("proj_out")
        gelu_in = sem("gelu_in")
        gelu_tanh = sem("gelu_tanh")
        v_ready = sem("v_ready")
        gate_in = sem("gate_in")
        gate_log = sem("gate_log")
        lf_ready = sem("lf_ready")
        ws_psum = sem("ws_psum")
        ws_t_ready = sem("ws_t_ready")
        ct_psum = sem("ct_psum")
        nct_ready = sem("nct_ready")
        mixed_psum = sem("mixed_psum")
        oa_ready = sem("oa_ready")
        oa_psum = sem("oa_psum")
        oa_hi = sem("oa_hi")
        oa_lo = sem("oa_lo")
        PROJ_TO = [km, vm, uv[:, :, 0:256], uv[:, :, 256:512], uv[:, :, 512:768], fqk[:, 0:2, :], fqk[:, 2:4, :],
                   fqk[:, 4:6, :], fv[:, :, 0:256], fv[:, :, 256:390], mq]
        PROJ_FEATURES = {0, 5, 6, 7, 10}

        def head_fox(h):
            r = (h % 2) * HD
            return Head(HM + h, lambda t: fqk[r:r + HD, h // 2, t * P:(t + 1) * P], lambda n: fqk[r:r + HD, 3 + h // 2, 0:n],
                        lambda s: fv[:, s, h * HD:(h + 1) * HD], lambda t: causal[:, 2 * P - t * P:3 * P],
                        lambda t: -0.125, 3 + h // 2, r, extra=(sel[:, h, :], lambda n: nct[:, 0:n]))

        def head_mem(h):
            r = (h % 2) * HD
            return Head(h, lambda t: mq[r:r + HD, h // 2, t * P:(t + 1) * P], lambda n: km[r:r + HD, h // 2, 0:n],
                        lambda s: vm[:, s, h * HD:(h + 1) * HD], lambda t: causal[:, 0:2 * P],
                        lambda t: -0.125, 6 + h // 2, r, causal=False)

        heads_m1 = [head_mem(h) for h in range(HM)] + [head_fox(h) for h in range(H1)]

        NBK, AH = 32, 16
        PAIRS = 1024
        CHUNKS = 64 * P // PAIRS
        STORE_LAG = 11
        window = arena[:, 9676:9868].bitcast(I32)
        table = arena[:, 9868:9996]
        table_hi, table_lo = act_lo[:, 0, 0:P], act_lo[:, 0, P:2 * P]
        edges = keep[:, 532:534]
        dist = scratch[:, 0:PAIRS].bitcast(I32)
        above = scratch[:, PAIRS:2 * PAIRS]
        hot = [act_hi[:, :, :].rearrange("p a b -> p (a b)")[:, 0:PAIRS],
               act_lo[:, :, :].rearrange("p a b -> p (a b)")[:, 2 * P:2 * P + PAIRS]]
        staged = [arena[:, S_AT:S_AT + PAIRS], junk]
        PITCH = 2 * P
        canvas = nc.dram_tensor("canvas", (AH, TT, P * (PITCH + 1) + 128), F32, kind="Internal").ap()
        rows = canvas[:, :, 0:P * PITCH].rearrange("h n (t s) -> h n t s", s=PITCH)
        skewed = canvas[:, :, 1:1 + P * (PITCH + 1)].rearrange("h n (t s) -> h n t s", s=PITCH + 1)
        window_landed = sem("window_landed")
        window_zero = sem("window_zero")
        table_zero = sem("table_zero")
        table_landed = sem("table_landed")
        table_hi_ready = sem("table_hi_ready")
        table_ready = sem("table_ready")
        neg_ready = sem("neg_ready")
        canvas_filled = sem("canvas_filled")
        canvas_written = [sem(f"canvas_written{n}") for n in range(2)]
        dist_ready = sem("dist_ready")
        hot_ready = sem("hot_ready")
        bias_psum = sem("bias_psum")
        bias_out = sem("bias_out")

        def dist_pool(c):
            if c:
                nc.gpsimd.wait_ge(hot_ready, c)
            w = window[:, 8 * c:8 * c + 8]
            key = bass.AP(tensor=w.tensor, offset=w.offset, ap=[list(w.ap[0]), [1, 8], [1, P]])
            query = window[:, 127 + 8 * c:135 + 8 * c].unsqueeze(2).to_broadcast([P, 8, P])
            nc.gpsimd.tensor_tensor(dist.rearrange("p (j u) -> p j u", j=8), query, key, ALU.subtract).then_inc(dist_ready, 1)

        def hot_vector(c):
            nc.vector.wait_ge(dist_ready, c + 1)
            if c >= 2:
                nc.vector.wait_ge(bias_psum, c - 1)
            dve_then(nc.vector.tensor_scalar(above, dist, edges[:, 0:1], None, ALU.is_ge))
            nc.vector.scalar_tensor_tensor(hot[c % 2], dist, edges[:, 1:2], above, ALU.is_lt, ALU.mult).then_inc(hot_ready, 1)

        def bias_tensor(c):
            nc.tensor.wait_ge(hot_ready, c + 1)
            if c >= 2:
                nc.tensor.wait_ge(bias_out, c - 1)
            for half in range(2):
                to, marks = ps[:, 2 * (c % 2) + half, :], hot[c % 2][:, half * 512:(half + 1) * 512]
                nc.tensor.matmul(to, table_hi, marks, start=True, stop=False, skip_group_check=True)
                last = nc.tensor.matmul(to, table_lo, marks, start=False, stop=True, skip_group_check=True)
            last.then_inc(bias_psum, 1)

        def bias_scalar(c):
            nc.scalar.wait_ge(bias_psum, c + 1)
            if c >= 2:
                nc.scalar.wait_ge(canvas_written[c % 2], 64 * (c // 2))
            nc.scalar.copy(staged[c % 2][0:64, :], ps[0:64, 2 * (c % 2):2 * (c % 2) + 2, :].rearrange("p b c -> p (b c)")).then_inc(bias_out, 1)

        def bias_store(c):
            nc.sync.wait_ge(bias_out, c + 1)
            if c == 0:
                nc.sync.wait_ge(canvas_filled, 96)
            for g in range(4):
                t0 = g % 2 * 64 + 8 * c
                nc.sync.dma_start(skewed[:, g // 2, t0:t0 + 8, 0:P],
                                    staged[c % 2][g * AH:(g + 1) * AH, :].rearrange("h (t u) -> h t u", t=8)).then_inc(canvas_written[c % 2], 16)

        qa = carve(0, TT, D)
        kva = carve(2048, TT, 256)
        kd = carve(2560, TT, 256)
        qt_a = carve(3072, 8, TOK)
        kt_a = carve(5120, 2, TOK)
        BR = 6
        bias = carve(5632, BR, 3 * P)
        sq_a = scratch[:, 0:1024].rearrange("p (b c) -> p b c", b=2)
        ss_a, rs_a = small[:, 0:40], small[:, 40:80]
        q_col, k_col = keep[:, 514:515], keep[:, 515:516]
        sinks = keep[:, 516:532]
        minus_sinks = small[:, 200:216]
        a_small = sem("a_small")
        a_out_ready = sem("a_out_ready")
        a_squares = sem("a_squares")
        a_sums = sem("a_sums")
        a_rstd = sem("a_rstd")
        a_scaled = sem("a_scaled")
        a_turned = sem("a_turned")
        a_turned_out = sem("a_turned_out")
        q_col_ready = sem("q_col_ready")
        bias_landed = [sem(f"bias_landed{n}") for n in range(BR)]
        E_A = len(heads_m1)
        A_TURN_BANK = [0, 1, 2, 6, 7]

        def bias_load(h):
            if h >= BR:
                nc.gpsimd.wait_ge(negmax_ready, E_A + h - BR + 1)
            nc.gpsimd.dma_start(bias[:, h % BR, 0:P], rows[h, 0, :, P:2 * P]).then_inc(bias_landed[h % BR], 16)
            nc.gpsimd.dma_start(bias[:, h % BR, P:3 * P], rows[h, 1, :, :]).then_inc(bias_landed[h % BR], 16)

        def head_a(h):
            r = (h % 2) * HD
            g = h // 8
            return Head(E_A + h, lambda t: qt_a[r:r + HD, h // 2, t * P:(t + 1) * P], lambda n: kt_a[r:r + HD, g, 0:n],
                        lambda s: kva[:, s, P + g * HD:P + (g + 1) * HD],
                        lambda t: bias[:, h % BR, t * P:3 * P if t else P], lambda t: -1.0, h // 2, r, sink=sinks[:, h:h + 1],
                        wait_tensor=lambda: nc.tensor.wait_ge(a_turned_out, 2 + h // 4), minus_sink=minus_sinks[:, h:h + 1],
                        wait_vector=lambda: nc.vector.wait_ge(bias_landed[h % BR], 32 * (h // BR + 1)))

        heads_a = [head_a(h) for h in range(AH)]

        BH, QK = 16, 96
        qb = carve(0, TT, BH * QK)
        kvb = carve(3072, TT, BH * P)
        qk_t = arena[0:QK, 7168:8192].rearrange("p (b c) -> p b c", b=2)
        c_gain = carve(8192, 384)
        flat_act = act[:, :, :].rearrange("p a b -> p (a b)")
        cb = flat_act[:, 0:832].rearrange("p (t c) -> p t c", t=TT)
        cn = arena[:, 9932:10700].rearrange("p (t c) -> p t c", t=TT)
        kc = scratch[:, :].rearrange("p (t h d) -> p t h d", t=TT, h=BH)
        ss_q, ss_k, minus_rs_q, rs_k = (small[:, 32 * n:32 * n + 32] for n in range(4))
        q_sq = [arena[:, 8704:10240], arena[:, 7168:8704]]
        EARLY = 10
        EARLY_KEYS = 8

        def q_at(t, h):
            return t * EARLY + h if h < EARLY else TT * EARLY + t * (BH - EARLY) + h - EARLY

        ss_c, rs_c = sums[:, 48:54], rstd[:, 48:52]
        cos, sin = (keep[:, 32 * n:32 * n + 32].rearrange("p (t c) -> p t c", t=TT) for n in range(2))
        gq, gk = keep[:, 64:160], keep[:, 160:256]
        qb_col, kb_col = keep[0:QK, 512:513], keep[0:QK, 513:514]
        rot = {name: keep[:, 256 + 32 * n:288 + 32 * n].rearrange("p (t c) -> p t c", t=TT)
               for n, name in enumerate(("q1c", "q2s", "q2c", "q1s", "k1c", "k2s", "k2c", "k1s"))}
        rope_at = [carve(3072 + 32 * n, TT, 16) for n in range(6)]
        pos_i = arena[:, 3264:3266].bitcast(I32)
        pos_f = arena[:, 3266:3268]
        freq = arena[:, 3268:3284]
        b_small = sem("b_small")
        pos_landed = sem("pos_landed")
        angle_ready = sem("angle_ready")
        sin_ready = sem("sin_ready")
        rot_ready = sem("rot_ready")
        c_out = sem("c_out")
        c_squares = sem("c_squares")
        c_rstd = sem("c_rstd")
        cn_ready = sem("cn_ready")
        c_turned = sem("c_turned")
        c_hi = sem("c_hi")
        c_lo = sem("c_lo")
        up_half = sem("up_half")
        up_scalar = sem("up_scalar")
        up_vector = sem("up_vector")
        q_squares = sem("q_squares")
        q_sums = sem("q_sums")
        k_squares = sem("k_squares")
        k_sums = sem("k_sums")
        qk_rstd = sem("qk_rstd")
        q_roped = sem("q_roped")
        q_roped_first = sem("q_roped_first")
        q_roped_late = sem("q_roped_late")
        kc_ready = sem("kc_ready")
        qk_psum = sem("qk_psum")
        qk_out = sem("qk_out")
        E_B = E_A + AH

        def head_b(h):
            def wait_tensor():
                nc.tensor.wait_ge(qk_out, h + 1)
            return Head(E_B + h, lambda t: qk_t[:, h % 2, t * P:(t + 1) * P], lambda n: qk_t[:, h % 2, TOK:TOK + n],
                        lambda s: kvb[:, s, h * P + HD:(h + 1) * P], lambda t: causal[:, 2 * P - t * P:3 * P],
                        lambda t: minus_rs_q[:, q_at(t, h):q_at(t, h) + 1], h // 2, (h % 2) * HD,
                        wait_tensor=wait_tensor, wait_vector={0: lambda: nc.vector.wait_ge(qk_rstd, 3), EARLY: lambda: nc.vector.wait_ge(qk_rstd, 4)}.get(h))

        heads_b = [head_b(h) for h in range(BH)]

        def turn_qk_tensor(h):
            if h >= BH:
                return
            if h >= 2:
                nc.tensor.wait_ge(qk_out, h - 1)
            if h == EARLY_KEYS:
                nc.tensor.wait_ge(kc_ready, 2 * TT)
            if h == EARLY:
                nc.tensor.wait_ge(q_roped_late, 1)
            for t in range(TT):
                nc.tensor.transpose(ps[0:QK, 6 + h % 2, t * P:(t + 1) * P], qb[:, t, h * QK:(h + 1) * QK], ident[:, :])
                last = nc.tensor.transpose(ps[0:QK, 6 + h % 2, TOK + t * P:TOK + (t + 1) * P], kc[:, t, h, :], ident[:, :])
            last.then_inc(qk_psum, 1)

        def turned_qk_scalar(h):
            if h >= BH:
                return
            nc.scalar.wait_ge(qk_psum, h + 1)
            if h >= 2:
                nc.scalar.wait_ge(scores_psum, E_B + h - 1)
            nc.scalar.activation(qk_t[:, h % 2, 0:TOK], ps[0:QK, 6 + h % 2, 0:TOK], ACT.Copy, scale=qb_col)
            nc.scalar.activation(qk_t[:, h % 2, TOK:2 * TOK], ps[0:QK, 6 + h % 2, TOK:2 * TOK], ACT.Copy, scale=kb_col).then_inc(qk_out, 1)

        def rope_queries(engine, then, tiles, h0, h1, buffers, done):
            for t in tiles:
                q = qb[:, t, :].rearrange("p (h d) -> p h d", h=BH)
                q1, q2 = q[:, h0:h1, HD:HD + 16], q[:, h0:h1, HD + 16:QK]
                a, b = buffers

                def turn(name):
                    return rot[name][:, t, :].unsqueeze(1).to_broadcast([P, h1 - h0, 16])

                engine.tensor_tensor(a, q1, turn("q1s"), ALU.mult)
                engine.tensor_tensor(b, q2, turn("q2s"), ALU.mult)
                engine.tensor_tensor(q1, q1, turn("q1c"), ALU.mult)
                then(engine.tensor_tensor(q2, q2, turn("q2c"), ALU.mult))
                engine.tensor_tensor(q1, q1, b, ALU.subtract)
                last = engine.tensor_tensor(q2, q2, a, ALU.add)
                if t != tiles[-1]:
                    then(last)
            last.then_inc(done, 1)

        tanh_ready = {st: sem(f"tanh_ready_{st}") for st in swiglu}
        half_ready = {st: sem(f"half_ready_{st}") for st in swiglu}
        hidden_ready = {st: sem(f"hidden_ready_{st}") for st in ("F0", "F1", "F2", "F3", "F4")}
        hidden_hi = {st: sem(f"hidden_hi_{st}") for st in hidden_ready}
        hidden_lo = {st: sem(f"hidden_lo_{st}") for st in hidden_ready}
        tanh_g = carve(0, 2, 512)
        half_g = carve(1024, 2, 512)

        def hidden_bank(bank):
            return lambda f: ps[:, bank, f * TOK:(f + 1) * TOK]

        def second_product(st, b, s, buf, begin, end, turn=0, per=0):
            nc.tensor.wait_ge(hidden_lo[st], s + 1 + per * turn)
            nc.tensor.wait_ge(lo_ready, b + 1 + RAW * turn)
            hi, lo = parts(b)
            for f, t in ((0, 0), (1, 0), (0, 1), (1, 1)) if end else ((0, 0), (0, 1), (1, 0), (1, 1)):
                c = f * TOK + t * P
                still = act_hi[:, buf, c:c + P], act_lo[:, buf, c:c + P]
                for half in range(2):
                    cols = slice(half * 512, (half + 1) * 512)
                    last = product(ps[:, 4 + 2 * t + half, :], still, (hi[:, f, cols], lo[:, f, cols]),
                                   begin and f == 0, end and f == 1)
                if end and (f, t) == (1, 0):
                    last.then_inc(y_tile, 1)
            last.then_inc(block_used, 1)

        def round_hidden(st, s, buf, down_block, turn=0, per=0):
            nc.scalar.wait_ge(hidden_ready[st], s + 1 + per * turn)
            if down_block is not None:
                nc.scalar.wait_ge(block_used, down_block + 1 + RAW * turn)
            nc.scalar.copy(act_hi[:, buf, :], act[:, buf, :]).then_inc(hidden_hi[st], 1)

        def split_hidden(st, s, buf, turn=0, per=0):
            nc.vector.wait_ge(hidden_hi[st], s + 1 + per * turn)
            nc.vector.tensor_tensor(act_lo[:, buf, :], act[:, buf, :], act_hi[:, buf, :].bitcast(F32),
                                    ALU.subtract).then_inc(hidden_lo[st], 1)

        def b_up(s):
            return first["F0"] + (2 * s - 1 if s else 0)

        def b_down(s):
            return first["F0"] + (2 * s + 2 if s < I0 - 1 else 2 * s + 1)

        def relu_tensor(s, turn=0):
            if s >= 3:
                nc.tensor.wait_ge(hidden_ready["F0"], s - 2 + 3 * turn)
            features_out(b_up(s), hidden_bank(s % 3), turn=turn, wait_h=8 if s == 0 else None)
            if s:
                second_product("F0", b_down(s - 1), s - 1, (s - 1) % 3, s == 1, False, turn, 3)

        relu_ready = sem("relu_ready")
        positive = carve(0, 3, 512)

        def relu_scalar(s, turn=0):
            nc.scalar.wait_ge(block_used, b_up(s) + 1 + RAW * turn)
            nc.scalar.activation(positive[:, s % 3, :], ps[:, s % 3, :], ACT.Relu).then_inc(relu_ready, 1)
            round_hidden("F0", s, s % 3, b_down(s - 3) if s >= 3 else None, turn, 3)
            if s:
                round_block(b_up(s) + 3, turn)
                round_block(b_up(s) + 4, turn)
            else:
                round_block(b_up(0) + 3)

        def relu_vector(s, turn=0):
            nc.vector.wait_ge(relu_ready, s + 1 + 3 * turn)
            nc.vector.tensor_tensor(act[:, s % 3, :], positive[:, s % 3, :], ps[:, s % 3, :], ALU.mult).then_inc(hidden_ready["F0"], 1)
            if s:
                split_block(b_up(s) + 3, turn)
            split_hidden("F0", s, s % 3, turn, 3)
            if s < I0 - 1:
                split_block(b_up(s) + (4 if s else 3), turn)

        def up_source(s):
            return i["w_ff1"][0].rearrange("(k p) n -> p k n", p=P)[:, :, bass.ds(256 * s, 256)]

        def rows_source(w, s):
            return w.rearrange("(s k p) n -> p s k n", k=2, p=P)[:, bass.ds(s, 1)].rearrange("p s k n -> p (s k) n")

        def relu_load(s, turn=0):
            load(b_up(s), up_source(s + 3 * turn), turn)
            if s:
                load(b_down(s - 1), rows_source(i["w_ff2"][0], s - 1 + 3 * turn), turn)

        RELU_PEEL, RELU_LAST = 4, 3

        def relu_steps(engine, step):
            for s in range(RELU_PEEL):
                step(s)
            with engine.Fori(0, (I0 - RELU_PEEL - RELU_LAST) // 3) as turn:
                for s in range(RELU_PEEL, RELU_PEEL + 3):
                    step(s, turn)
            for s in range(I0 - RELU_LAST, I0):
                step(s)

        def b_gate(st, s):
            return first[st] + (3 * s - 1 if s else 0)

        def b_upper(st, s):
            return first[st] + (3 * s if s else 1)

        def b_lower(st, s):
            return first[st] + (3 * s + 4 if s < I1 - 1 else 3 * s + 2)

        def column_source(w, s):
            return w.rearrange("(k p) n -> p k n", p=P)[:, :, bass.ds(256 * s, 256)]

        def swiglu_load(st, s, turn=0):
            wg, wu, wd = swiglu_weights(st)
            load(b_gate(st, s), column_source(wg, s + 2 * turn), turn)
            load(b_upper(st, s), column_source(wu, s + 2 * turn), turn)
            if s:
                load(b_lower(st, s - 1), rows_source(wd, s - 1 + 2 * turn), turn)

        def swiglu_tensor(st, n, s, turn=0):
            if s >= 2:
                nc.tensor.wait_ge(hidden_ready[st], s - 1 + 2 * turn)
            features_out(b_gate(st, s), hidden_bank(s % 2), turn=turn, wait_h=4 * n if s == 0 else None)
            features_out(b_upper(st, s), hidden_bank(2 + s % 2), turn=turn)
            if s:
                second_product(st, b_lower(st, s - 1), s - 1, (s - 1) % 2, s == 1, False, turn, 2)

        def swiglu_scalar(st, s, turn=0):
            nc.scalar.wait_ge(block_used, b_gate(st, s) + 1 + RAW * turn)
            nc.scalar.activation(tanh_g[:, s % 2, :], ps[:, s % 2, :], ACT.Tanh, scale=0.5).then_inc(tanh_ready[st], 1)
            round_block(b_gate(st, s) + 3, turn)
            round_block(b_upper(st, s) + 3, turn)
            round_hidden(st, s, s % 2, b_lower(st, s - 2) if s >= 2 else None, turn, 2)
            if s:
                round_block(b_upper(st, s) + 4, turn)

        def swiglu_vector(st, s, turn=0):
            nc.vector.wait_ge(tanh_ready[st], s + 1 + 2 * turn)
            nc.vector.scalar_tensor_tensor(half_g[:, s % 2, :], tanh_g[:, s % 2, :], 1.0, ps[:, s % 2, :],
                                           ALU.add, ALU.mult).then_inc(half_ready[st], 1)
            split_block(b_gate(st, s) + 3, turn)
            nc.vector.wait_ge(block_used, b_upper(st, s) + 1 + RAW * turn)
            nc.vector.wait_ge(half_ready[st], s + 1 + 2 * turn)
            nc.vector.scalar_tensor_tensor(act[:, s % 2, :], half_g[:, s % 2, :], 0.5, ps[:, 2 + s % 2, :],
                                           ALU.mult, ALU.mult).then_inc(hidden_ready[st], 1)
            split_block(b_upper(st, s) + 3, turn)
            split_hidden(st, s, s % 2, turn, 2)
            if 0 < s < I1 - 1:
                split_block(b_upper(st, s) + 4, turn)

        SWIGLU_PEEL, SWIGLU_LAST = 3, 2

        def swiglu_steps(engine, st, step):
            for s in range(SWIGLU_PEEL):
                step(st, s)
            with engine.Fori(0, (I1 - SWIGLU_PEEL - SWIGLU_LAST) // 2) as turn:
                for s in range(SWIGLU_PEEL, SWIGLU_PEEL + 2):
                    step(st, s, turn)
            for s in range(I1 - SWIGLU_LAST, I1):
                step(st, s)

        block = ctx.enter_context(nc.Block())

        @block.gpsimd
        def _(pool):
            pool_then(nc.gpsimd.memset(ident[:, :], 1.0))
            pool_then(nc.gpsimd.affine_select(out=ident[:, :], in_=ident[:, :], compare_op=ALU.is_equal, fill=0.0,
                                              base=0, pattern=[[-1, P]], channel_multiplier=1))
            pool_then(nc.gpsimd.memset(tri[:, 0:P], 0.0))
            pool_then(nc.gpsimd.memset(tri[:, P:3 * P], 1.0))
            pool_then(nc.gpsimd.affine_select(out=tri[:, P:2 * P], in_=tri[:, P:2 * P], compare_op=ALU.is_ge, fill=0.0,
                                              base=0, pattern=[[1, P]], channel_multiplier=-1))
            pool_then(nc.gpsimd.memset(causal[:, :], 0.0))
            nc.gpsimd.affine_select(out=causal[:, 2 * P:3 * P], in_=causal[:, 2 * P:3 * P], compare_op=ALU.is_ge, fill=NEG,
                                    base=0, pattern=[[-1, P]], channel_multiplier=1).then_inc(tables_ready, 1)
            pool_then(nc.gpsimd.memset(halves[:, :], -0.5))
            nc.gpsimd.memset(window, 0).then_inc(window_zero, 1)
            nc.gpsimd.memset(table, 0.0).then_inc(table_zero, 1)
            norm_pool(0)
            norm_pool(1)
            nc.gpsimd.memset(act[:, :, :], NEG).then_inc(neg_ready, 1)
            pool.wait_ge(neg_ready, 1)
            fill = canvas.rearrange("h n c -> (h n c)").rearrange("(p c) -> p c", p=P)
            NF = fill.shape[1] // 6
            for n in range(6):
                nc.gpsimd.dma_start(fill[:, n * NF:(n + 1) * NF],
                                    act[:, :, :].rearrange("p a b -> p (a b)")[:, 0:NF]).then_inc(canvas_filled, 16)
            pool.wait_ge(window_landed, 64)
            pool.wait_ge(gain_psum, 1)
            dist_pool(0)
            dist_pool(1)
            pool_then(nc.gpsimd.memset(sel[:, :, :], 1.0))
            nc.gpsimd.affine_select(out=sel[:, :, :], in_=sel[:, :, :], compare_op=ALU.is_equal, fill=0.0,
                                    base=0, pattern=[[-1, H1], [0, P]], channel_multiplier=1).then_inc(tables_ready, 1)
            pool.wait_ge(small_landed, 32)
            nc.gpsimd.affine_select(out=ws, in_=ws, compare_op=ALU.is_ge, fill=0.0,
                                    base=0, pattern=[[0, G], [-1, P]], channel_multiplier=1).then_inc(ws_ready, 1)
            for c in range(2, CHUNKS):
                dist_pool(c)
            pool.wait_ge(v_sumsq, 1)
            rsqrt_pool(rsv, ssv, HD, v_rstd)
            add_normed_pool(0)
            if "F0" in STAGES:
                norm_pool(2)
                add_normed_pool(1)
            if "F1" in STAGES:
                norm_pool(3)
            if "MA" in STAGES:
                pool.wait_ge(x_ready, 2)
                nc.gpsimd.dma_start(sinks, i["a_sinks_2"][0:1, :].to_broadcast([P, AH])).then_inc(a_small, 16)
                for r in range(2):
                    rows_of = slice(r * HD, (r + 1) * HD)
                    nc.gpsimd.dma_start(q_col[rows_of, :], i["a_q_gain_2"].rearrange("a n -> n a"), allow_slow_non_contiguous=True).then_inc(a_small, 16)
                    nc.gpsimd.dma_start(k_col[rows_of, :], i["a_k_gain_2"].rearrange("a n -> n a"), allow_slow_non_contiguous=True).then_inc(a_small, 16)
                for n in range(2):
                    pool.wait_ge(canvas_written[n], 32 * CHUNKS)
                for h in range(BR):
                    bias_load(h)
                norm_pool(4)
                for p in range(5):
                    pool.wait_ge(a_sums, p + 1)
                    rsqrt_pool(rs_a[:, 8 * p:8 * p + 8], ss_a[:, 8 * p:8 * p + 8], HD, a_rstd)
                for h in range(BR, AH):
                    bias_load(h)
            if "F2" in STAGES:
                norm_pool(5)
            if "F3" in STAGES:
                norm_pool(6)
            if "MB" in STAGES:
                pool_then(nc.gpsimd.memset(qb_col, 1.0))
                pool_then(nc.gpsimd.memset(kb_col, 1.0))
                nc.gpsimd.dma_start(qb_col[0:HD, :], i["b_q_gain_2"][:, 0:HD].rearrange("a n -> n a"), allow_slow_non_contiguous=True).then_inc(b_small, 16)
                nc.gpsimd.dma_start(kb_col[0:HD, :], i["b_k_gain_2"][:, 0:HD].rearrange("a n -> n a"), allow_slow_non_contiguous=True).then_inc(b_small, 16)
                pool.wait_ge(x_ready, 8)
                nc.gpsimd.dma_start(c_gain[:, 0:256], i["b_q_norm_2"].to_broadcast([P, 256])).then_inc(b_small, 16)
                nc.gpsimd.dma_start(c_gain[:, 256:384], i["b_kv_norm_2"].to_broadcast([P, P])).then_inc(b_small, 16)
                norm_pool(7)
                pool.wait_ge(c_squares, 2)
                rsqrt_pool(rs_c[:, 2:4], ss_c[:, 2:4], P, c_rstd)
                pool.wait_ge(c_squares, 6)
                rsqrt_pool(rs_c[:, 0:2], ss_c[:, 0:2], 256, c_rstd)
                for t in range(TT):
                    pool.wait_ge(k_sums, t + 1)
                    rsqrt_pool(rs_k[:, t * BH:(t + 1) * BH], ss_k[:, t * BH:(t + 1) * BH], QK, qk_rstd)
                pool.wait_ge(rot_ready, 1)
                pool.wait_ge(q_squares, 1)
                pool.wait_ge(up_scalar, 2)
                n = EARLY * 16
                rope_queries(nc.gpsimd, pool_then, (0,), 0, EARLY,
                             [flat_act[:, a:a + n].rearrange("p (h c) -> p h c", c=16) for a in (0, n)], q_roped_first)
                pool.wait_ge(q_sums, 1)
                early = slice(0, TT * EARLY)
                rsqrt_pool(minus_rs_q[:, early], ss_q[:, early], 1, qk_rstd, eps=QK * EPS, negate=True)
                pool.wait_ge(q_sums, 2)
                late = slice(TT * EARLY, TT * BH)
                rsqrt_pool(minus_rs_q[:, late], ss_q[:, late], 1, qk_rstd, eps=QK * EPS, negate=True)
                n = (BH - EARLY) * 16
                rope_queries(nc.gpsimd, pool_then, (0, 1), EARLY, BH,
                             [flat_act[:, 832 + a:832 + a + n].rearrange("p (h c) -> p h c", c=16) for a in (0, n)], q_roped_late)
            if "F4" in STAGES:
                norm_pool(8)

        @block.sync
        def _(sp):
            for t in range(TT):
                sp.dma_start(mem[:, t, :], i["mem"][0][t * P:(t + 1) * P, :]).then_inc(mem_landed[t], 16)
            row = 0
            for source in gain_sources:
                n = source.shape[0] * KD
                sp.dma_start(gain_rows[row:row + n, :], source.rearrange("a (k p) -> (a k) p", p=P)).then_inc(gain_landed, 16)
                row += n
            load(0)
            load(1)
            sp.dma_start(x[:, :, :], i["x"][0].rearrange("(t p) d -> p t d", p=P)).then_inc(x_landed, 16)
            load(2)
            sp.wait_ge(table_zero, 1)
            for g in range(4):
                sp.dma_start(table[g * NBK:(g + 1) * NBK, g * AH:(g + 1) * AH], i["rel_bias_2"]).then_inc(table_landed, 16)
            sp.dma_start(edges, i["bucket_edges"]).then_inc(table_landed, 16)
            sp.wait_ge(window_zero, 1)
            for g in range(4):
                skip = max(0, 127 - 64 * g)
                n = 191 - skip
                s0 = 64 * g - 127 + skip
                sp.dma_start(window[g * NBK:(g + 1) * NBK, skip:191],
                             i["positions_2"][0:1, s0:s0 + n].to_broadcast([NBK, n])).then_inc(window_landed, 16)
            sp.dma_start(pos_i, i["positions_2"].rearrange("a (t p) -> p (a t)", p=P), allow_slow_non_contiguous=True).then_inc(pos_landed, 16)
            sp.dma_start(freq, i["rope_freq"].to_broadcast([P, 16])).then_inc(pos_landed, 16)
            sp.dma_start(gq, i["b_q_gain_2"][0:1, :].to_broadcast([P, QK])).then_inc(pos_landed, 16)
            sp.dma_start(gk, i["b_k_gain_2"][0:1, :].to_broadcast([P, QK])).then_inc(pos_landed, 16)
            load(3)
            sp.dma_start(ws, i["gmlp_w_s"][0].rearrange("g t s -> t g s")).then_inc(small_landed, 16)
            sp.dma_start(bs, i["gmlp_b_s"][0]).then_inc(small_landed, 16)
            sp.dma_start(bf, i["b_forget"][0:1, :].to_broadcast([P, H1])).then_inc(bf_landed, 16)
            sp.dma_start(vgain, i["gmlp_v_norm"][0:1, :].to_broadcast([P, 384])).then_inc(vgain_landed, 16)
            for b in range(4, first["F0"]):
                load(b)
                if b == 8:
                    sp.dma_start(post_gain[:, :], i["norm_post_mix"].to_broadcast([P, D])).then_inc(post_gain_landed, 16)
            if "F0" in STAGES:
                relu_steps(sp, relu_load)
                load(b_down(I0 - 1))
                sp.wait_ge(x_ready, 2)
                sp.dma_start(post_gain[:, :], i["norm_post_ffn"].to_broadcast([P, D])).then_inc(post_gain_landed, 16)
            if "F1" in STAGES:
                swiglu_steps(sp, "F1", swiglu_load)
                load(b_lower("F1", I1 - 1))

            if "MA" in STAGES:
                for b in range(first["a_in"], first["a_out"] + 4):
                    load(b)
            if "F2" in STAGES:
                swiglu_steps(sp, "F2", swiglu_load)
                load(b_lower("F2", I1 - 1))
                swiglu_steps(sp, "F3", swiglu_load)
                load(b_lower("F3", I1 - 1))
            if "MB" in STAGES:
                for b in range(first["b_in"], first["b_out"] + 4):
                    load(b)
            if "F4" in STAGES:
                swiglu_steps(sp, "F4", swiglu_load)
                load(b_lower("F4", I1 - 1))
            for t in range(TT):
                sp.wait_ge(x_ready, 2 * (len(STAGES) - 1) + t + 1)
                sp.dma_start(out[t * P:(t + 1) * P, :], x[:, t, :]).then_inc(out_landed, 16)
            sp.wait_ge(out_landed, 32)

        @block.scalar
        def _(scalar):
            norm_scalar_sums(0, mem, lambda e, t: e.wait_ge(mem_landed[t], 16))
            round_block(0)
            scalar.wait_ge(gain_psum, 1)
            nc.scalar.copy(gain_col[:, :], ps[:, 7, 0:GAIN_ROWS]).then_inc(gain_ready, 1)
            scalar.wait_ge(gain_ready, 1)
            norm_scalar_round(0)
            round_block(1)
            norm_scalar_sums(1, x, lambda e, t: e.wait_ge(x_landed, 16))
            round_block(2)

            def project_out(p):
                scalar.wait_ge(block_used, first["kv"] + p + 1)
                to = PROJ_TO[p]
                n = to.shape[2]
                nc.scalar.copy(to, ps[:, 4 + p % 4, :].rearrange("p (a b) -> p a b", a=2)[:, :, 0:n]).then_inc(proj_out, 1)

            for p in range(11):
                if p == 10:
                    scalar.wait_ge(gate_in, 1)
                    act_then(nc.scalar.activation(ge, gaz, ACT.Exp))
                    nc.scalar.activation(ge, ge, ACT.Ln, bias=1.0).then_inc(gate_log, 1)
                project_out(p)
                if p == 1:
                    norm_scalar_round(1)
                round_block(p + 3)
                if p == 1:
                    scalar.wait_ge(table_landed, 80)
                    nc.scalar.copy(table_hi, table).then_inc(table_hi_ready, 1)
                if p == 3:
                    scalar.wait_ge(angle_ready, 1)
                    nc.scalar.activation(sin, rope_at[4], ACT.Sin).then_inc(sin_ready, 1)
                    nc.scalar.activation(cos, rope_at[5], ACT.Sin).then_inc(sin_ready, 1)
                if 3 <= p < 3 + CHUNKS:
                    bias_scalar(p - 3)
                if p == 7:
                    scalar.wait_ge(gelu_in, 1)
                    nc.scalar.activation(g1, g1, ACT.Tanh, scale=0.7978845608028654).then_inc(gelu_tanh, 1)
            scalar.wait_ge(ws_psum, 1)
            nc.scalar.copy(ws_t[:, 0:4, :], ps[:, 7, :].rearrange("p (g t) -> p g t", g=4)).then_inc(ws_t_ready, 1)
            nc.scalar.copy(ws_t[:, 4:6, :], ps[:, 5, 0:256].rearrange("p (g t) -> p g t", g=2)).then_inc(ws_t_ready, 1)
            nc.scalar.copy(bs_t, ps[:, 5, 256:262]).then_inc(ws_t_ready, 1)
            scalar.wait_ge(ct_psum, 1)
            nc.scalar.activation(nct, ps[0:6, 4, 0:256], ACT.Copy, scale=-8.0).then_inc(nct_ready, 1)

            def gated_round(n):
                if n == 5:
                    scalar.wait_ge(oa_psum, 1)
                    nc.scalar.copy(h_hi[:, 0:2, :], ps[:, 6, :].rearrange("p (k t) -> p k t", k=2)).then_inc(oa_hi, 1)
                    nc.scalar.copy(h_hi[:, 2, :], ps[:, 7, 0:256]).then_inc(oa_hi, 1)

            attention_scalar(heads_m1, gated_round)
            for b in range(first["out"], first["out"] + 3):
                round_block(b + 3)
            scalar.wait_ge(canvas_written[1], 32 * CHUNKS)
            def norm_scalar(n, r, late):
                norm_scalar_sums(n, x, x_after(r))
                round_block(late)
                norm_scalar_round(n)

            add_normed_scalar(0, 0)
            if "F0" in STAGES:
                norm_scalar(2, 0, first["out"] + 6)
                relu_steps(scalar, relu_scalar)
                add_normed_scalar(1, 1)

            def late_block(st):
                return first[st] + 3 * I1 + 2

            def ffn_scalar(st, n, r, late):
                norm_scalar(n, r - 1, late)
                swiglu_steps(scalar, st, swiglu_scalar)

            if "F1" in STAGES:
                ffn_scalar("F1", 3, 2, first["F0"] + 2 * I0 + 2)
            if "MA" in STAGES:
                norm_scalar(4, 2, late_block("F1"))

                def turned_a(p):
                    scalar.wait_ge(a_turned, p + 1)
                    if p == 0:
                        scalar.wait_ge(a_small, 80)
                        scalar.wait_ge(q_col_ready, 1)
                    to = qt_a[:, 2 * p - 2:2 * p, :] if p else kt_a[:, :, :]
                    nc.scalar.activation(to, ps[:, A_TURN_BANK[p], :].rearrange("p (k t) -> p k t", k=2), ACT.Copy,
                                         scale=q_col if p else k_col).then_inc(a_turned_out, 1)

                for p in range(5):
                    b = first["a_in"] + p
                    scalar.wait_ge(block_used, b + 1)
                    bank = ps[:, 4 + p % 4, :]
                    to = qa[:, :, 256 * p - 256:256 * p] if p else kva
                    nc.scalar.copy(to, bank.rearrange("p (t c) -> p t c", t=TT)).then_inc(a_out_ready, 1)
                    if p >= 2:
                        scalar.wait_ge(a_sums, p - 1)
                    nc.scalar.activation(sq_a[:, p % 2, :], bank, ACT.Square).then_inc(a_squares, 1)
                    if p < 4:
                        round_block(b + 3)
                    if p >= 2:
                        turned_a(p - 2)
                round_block(first["a_in"] + 7)
                attention_scalar(heads_a, lambda n: turned_a(n + 2) if n in (1, 2) else None)
                for b in range(first["a_out"], first["a_out"] + 3):
                    round_block(b + 3)
            if "F2" in STAGES:
                ffn_scalar("F2", 5, 4, first["a_out"] + 6)
                ffn_scalar("F3", 6, 5, late_block("F2"))
            if "MB" in STAGES:
                norm_scalar(7, 5, late_block("F3"))
                junk_free()
                counted = 0
                for p, (kinds, c0, w) in enumerate(((((2, 256, 384), (4, 384, 416)), 256, 160), (((0, 0, 256),), 0, 256))):
                    b = first["b_in"] + p
                    scalar.wait_ge(block_used, b + 1)
                    bank = ps[:, 4 + p, :].rearrange("p (t c) -> p t c", t=TT)
                    nc.scalar.copy(cb[:, :, c0:c0 + w], bank[:, :, 0:w]).then_inc(c_out, 1)
                    for at, begin, end in kinds:
                        for t in range(TT):
                            if t:
                                scalar.wait_ge(c_squares, counted)
                            counted += 1
                            nc.scalar.activation(junk[:, begin:end], bank[:, t, begin - c0:end - c0], ACT.Square,
                                                 accum_out=ss_c[:, at + t:at + t + 1]).then_inc(c_squares, 1)
                    if p:
                        scalar.wait_ge(c_turned, 1)
                        nc.scalar.copy(h_hi[:, 2, :], ps[:, 7, 0:TOK]).then_inc(c_hi, 1)
                    round_block(b + 3)
                up = first["b_up"]

                def heads_of(ap):
                    return ap.rearrange("p (h c) -> p h c", h=BH)[:, :, 0:HD]

                scalar.wait_ge(up_half, 1)
                bank = ps[:, 0:4, :].rearrange("p b c -> p (b c)")
                nc.scalar.copy(kvb[:, 0, :], bank).then_inc(up_scalar, 1)
                nc.scalar.activation(kc[:, 0, :, 0:HD], heads_of(bank), ACT.Square).then_inc(k_squares, 1)
                scalar.wait_ge(c_turned, 2)
                nc.scalar.copy(h_hi[:, 0:2, :], ps[:, 0, :].rearrange("p (k t) -> p k t", k=2)).then_inc(c_hi, 1)
                scalar.wait_ge(up_vector, 1)
                scalar.wait_ge(c_squares, 6)
                nc.scalar.activation(kc[:, 1, :, 0:HD], heads_of(kvb[:, 1, :]), ACT.Square).then_inc(k_squares, 1)
                for t in range(TT):
                    if t:
                        scalar.wait_ge(block_used, up + 2)
                    else:
                        scalar.wait_ge(up_half, 2)
                    bank = ps[:, 2 + 2 * t:4 + 2 * t, :].rearrange("p b c -> p (b c)")
                    nc.scalar.copy(qb[:, t, 0:1024], bank).then_inc(up_scalar, 1)
                    nc.scalar.activation(q_sq[t][:, 0:1024], bank, ACT.Square).then_inc(q_squares, 1)
                scalar.wait_ge(block_used, up + 3)
                nc.scalar.copy(qb[:, :, 1024:1536], ps[:, 0:2, :]).then_inc(up_scalar, 1)
                for t in range(TT):
                    nc.scalar.activation(q_sq[t][:, 1024:1536], ps[:, t, :], ACT.Square).then_inc(q_squares, 1)
                round_block(up + 3)
                round_block(up + 4)
                scalar.wait_ge(q_sums, 2)
                scalar.wait_ge(b_small, 64)
                turned_qk_scalar(0)
                turned_qk_scalar(1)
                round_block(up + 5)
                attention_scalar(heads_b, lambda n: turned_qk_scalar(n + 2))
                for b in range(first["b_out"], first["b_out"] + 3):
                    round_block(b + 3)
            if "F4" in STAGES:
                ffn_scalar("F4", 8, 7, first["b_out"] + 6)

        @block.vector
        def _(vector):
            def angles():
                vector.wait_ge(pos_landed, 64)
                dve_then(nc.vector.tensor_copy(pos_f, pos_i))
                ang, turns, low, high, sin_in, cos_in = rope_at
                for t in range(TT):
                    last = nc.vector.tensor_scalar(ang[:, t, :], freq, pos_f[:, t:t + 1], None, ALU.mult)
                dve_then(last)
                dve_then(nc.vector.tensor_scalar(turns, ang, 0.15915494309189535, 12582912.0, ALU.mult, ALU.add))
                dve_then(nc.vector.tensor_scalar(turns, turns, -12582912.0, None, ALU.add))
                dve_then(nc.vector.scalar_tensor_tensor(low, turns, -6.28125, ang, ALU.mult, ALU.add))
                dve_then(nc.vector.scalar_tensor_tensor(low, turns, -0.0019353071795864769, low, ALU.mult, ALU.add))
                dve_then(nc.vector.tensor_scalar(high, low, 1.5707963267948966, -6.283185307179586, ALU.is_gt, ALU.mult))
                dve_then(nc.vector.scalar_tensor_tensor(high, low, 1.5707963267948966, high, ALU.add, ALU.add))
                nc.vector.tensor_scalar(sin_in, low, 3.1415925, -3.1415925, ALU.min, ALU.max)
                nc.vector.tensor_scalar(cos_in, high, 3.1415925, -3.1415925, ALU.min, ALU.max).then_inc(angle_ready, 1)

            norm_vector_diag(0)
            split_block(0)
            norm_vector_split(0)
            split_block(1)
            norm_vector_diag(1)
            split_block(2)

            def gelu(part):
                both = uv[:, :, :].rearrange("p t c -> p (t c)")
                v = uv[:, :, 384:768]
                if part == 0:
                    vector.wait_ge(proj_out, 5)
                    vector.wait_ge(canvas_filled, 96)
                    dve_then(nc.vector.tensor_tensor(g1, both, both, ALU.mult))
                    dve_then(nc.vector.tensor_scalar(g1, g1, 0.044715, 1.0, ALU.mult, ALU.add))
                    nc.vector.tensor_tensor(g1, g1, both, ALU.mult).then_inc(gelu_in, 1)
                if part == 1:
                    vector.wait_ge(gelu_tanh, 1)
                    dve_then(nc.vector.scalar_tensor_tensor(both, g1, 1.0, both, ALU.add, ALU.mult))
                    dve_then(nc.vector.tensor_scalar(both, both, 0.5, None, ALU.mult))
                if part == 2:
                    sq = act[:, 0:2, 0:384]
                    dve_then(nc.vector.tensor_tensor(sq, v, v, ALU.mult))
                    for t in range(TT):
                        last = nc.vector.tensor_reduce(ssv[:, t * G:(t + 1) * G], sq[:, t, :].rearrange("p (g d) -> p g d", g=G), AX.X, ALU.add)
                    last.then_inc(v_sumsq, 1)
                if part == 3:
                    vector.wait_ge(v_rstd, 1)
                    for t in range(TT):
                        last = nc.vector.tensor_tensor(v[:, t, :].rearrange("p (g d) -> p g d", g=G), v[:, t, :].rearrange("p (g d) -> p g d", g=G),
                                                       rsv[:, t * G:(t + 1) * G].to_broadcast([P, G, HD]), ALU.mult)
                    dve_then(last)
                    vector.wait_ge(vgain_landed, 16)
                    for t in range(TT):
                        last = nc.vector.tensor_tensor(v[:, t, :], v[:, t, :], vgain, ALU.mult)
                    last.then_inc(v_ready, 1)

            for p in range(11):
                if p == 1:
                    norm_vector_split(1)
                if p == 9:
                    vector.wait_ge(bf_landed, 16)
                    vector.wait_ge(proj_out, 10)
                    for t in range(TT):
                        last = nc.vector.tensor_tensor(gz[:, t, :], fv[:, t, 384:390], bf, ALU.add)
                    dve_then(last)
                    nc.vector.tensor_scalar(gmin, gz, 0.0, None, ALU.min)
                    nc.vector.scalar_tensor_tensor(gaz, gz, -1.0, gz, ALU.mult, ALU.min).then_inc(gate_in, 1)
                if 2 <= p < 1 + CHUNKS:
                    hot_vector(p - 1)
                split_block(p + 3)
                if p == 1:
                    hot_vector(0)
                    vector.wait_ge(table_hi_ready, 1)
                    nc.vector.tensor_tensor(table_lo, table, table_hi.bitcast(F32), ALU.subtract).then_inc(table_ready, 1)
                if p == 2:
                    angles()
                if p == 4:
                    vector.wait_ge(sin_ready, 2)
                    for name, (g, at, by) in {"q1c": (gq, 0, cos), "q2s": (gq, 16, sin), "q2c": (gq, 16, cos), "q1s": (gq, 0, sin),
                                              "k1c": (gk, 0, cos), "k2s": (gk, 16, sin), "k2c": (gk, 16, cos), "k1s": (gk, 0, sin)}.items():
                        last = nc.vector.tensor_tensor(rot[name], by, g[:, HD + at:HD + at + 16].unsqueeze(1).to_broadcast([P, TT, 16]), ALU.mult)
                    last.then_inc(rot_ready, 1)
                if p == 5:
                    gelu(0)
                if p == 8:
                    gelu(1)
                    gelu(2)
                if p == 9:
                    vector.wait_ge(gate_log, 1)
                    nc.vector.tensor_tensor(lf, gmin, ge, ALU.subtract).then_inc(lf_ready, 1)
                    gelu(3)

            def gated_split(n):
                if n == 2:
                    vector.wait_ge(mixed_psum, 1)
                    for t in range(TT):
                        for g in range(G):
                            c = slice(g * HD, (g + 1) * HD)
                            last = nc.vector.scalar_tensor_tensor(oa[:, t, c], ps[:, 6 + t, c], bs_t[:, g:g + 1], uv[:, t, c], ALU.add, ALU.mult)
                    last.then_inc(oa_ready, 1)
                if n == 6:
                    for a, (h, bank) in enumerate(((slice(0, 2), ps[:, 6, :]), (slice(2, 3), ps[:, 7, 0:256]))):
                        vector.wait_ge(oa_hi, a + 1)
                        nc.vector.tensor_tensor(h_lo[:, h, :], bank.rearrange("p (k t) -> p k t", t=TOK), h_hi[:, h, :].bitcast(F32),
                                                ALU.subtract).then_inc(oa_lo, 1)

            vector.wait_ge(canvas_written[0], 32 * CHUNKS)
            attention_vector(heads_m1, gated_split)
            for b in range(first["out"], first["out"] + 2):
                split_block(b + 3)
            add_normed_vector(0)

            def norm_vector(n, late):
                norm_vector_diag(n)
                norm_vector_split(n)
                split_block(late - 1)
                split_block(late)

            if "F0" in STAGES:
                norm_vector(2, first["out"] + 6)
                relu_steps(vector, relu_vector)
                add_normed_vector(1)

            def late_block(st):
                return first[st] + 3 * I1 + 2

            def ffn_vector(st, n, r, late):
                norm_vector(n, late)
                swiglu_steps(vector, st, swiglu_vector)
                add_scaled(r, 0.5)

            if "F1" in STAGES:
                ffn_vector("F1", 3, 2, first["F0"] + 2 * I0 + 2)
            if "MA" in STAGES:
                norm_vector(4, late_block("F1"))
                vector.wait_ge(a_small, 80)
                nc.vector.tensor_scalar(q_col, q_col, 0.125, None, ALU.mult).then_inc(q_col_ready, 1)
                dve_then(nc.vector.tensor_scalar(minus_sinks, sinks, -1.0, None, ALU.mult))

                def scale_heads(p):
                    vector.wait_ge(a_rstd, p + 1)
                    for t in range(TT):
                        rs = rs_a[:, 8 * p + 4 * t:8 * p + 4 * t + 4]
                        if p:
                            v = qa[:, t, 256 * p - 256:256 * p].rearrange("p (h d) -> p h d", h=4)
                            last = nc.vector.tensor_tensor(v, v, rs.unsqueeze(2).to_broadcast([P, 4, HD]), ALU.mult)
                        else:
                            for twin in range(2):
                                last = nc.vector.tensor_tensor(kd[:, t, :].rearrange("p (g w d) -> p g w d", g=2, w=2)[:, :, twin, :],
                                                               kva[:, t, 0:P].rearrange("p (g d) -> p g d", g=2),
                                                               rs[:, 0:2].unsqueeze(2).to_broadcast([P, 2, HD]), ALU.mult)
                    last.then_inc(a_scaled, 1)

                for p in range(5):
                    vector.wait_ge(a_squares, p + 1)
                    nc.vector.tensor_reduce(ss_a[:, 8 * p:8 * p + 8], sq_a[:, p % 2, :].rearrange("p (h d) -> p h d", h=8),
                                            AX.X, ALU.add).then_inc(a_sums, 1)
                    if p < 4:
                        split_block(first["a_in"] + p + 3)
                    if p:
                        scale_heads(p - 1)
                split_block(first["a_in"] + 7)
                attention_vector(heads_a, lambda n: scale_heads(4) if n == 1 else None)
                for b in range(first["a_out"], first["a_out"] + 2):
                    split_block(b + 3)
                add_scaled(3, 1.0)
            if "F2" in STAGES:
                ffn_vector("F2", 5, 4, first["a_out"] + 6)
                ffn_vector("F3", 6, 5, late_block("F2"))
            if "MB" in STAGES:
                norm_vector(7, late_block("F3"))
                vector.wait_ge(b_small, 64)

                def latent(n, at, cols):
                    vector.wait_ge(c_rstd, n)
                    vector.wait_ge(c_out, n)
                    for t in range(TT):
                        last = nc.vector.scalar_tensor_tensor(cn[:, t, cols], cb[:, t, cols], rs_c[:, at + t:at + t + 1],
                                                              c_gain[:, cols], ALU.mult, ALU.mult)
                    last.then_inc(cn_ready, 1)

                def split_latent(n, h, bank):
                    vector.wait_ge(c_hi, n)
                    nc.vector.tensor_tensor(h_lo[:, h, :], bank.rearrange("p (k t) -> p k t", t=TOK), h_hi[:, h, :].bitcast(F32),
                                            ALU.subtract).then_inc(c_lo, 1)

                latent(1, 2, slice(256, 384))
                split_block(first["b_in"] + 3)
                split_latent(1, slice(2, 3), ps[:, 7, 0:TOK])
                latent(2, 0, slice(0, 256))
                kr = [cb[:, :, 384 + 16 * n:400 + 16 * n] for n in range(2)]
                ks = [flat_act[:, 832 + 32 * n:864 + 32 * n].rearrange("p (t c) -> p t c", t=TT) for n in range(2)]
                nc.vector.tensor_tensor(ks[0], kr[0], rot["k1s"], ALU.mult)
                nc.vector.tensor_tensor(ks[1], kr[1], rot["k2s"], ALU.mult)
                nc.vector.tensor_tensor(kr[0], kr[0], rot["k1c"], ALU.mult)
                dve_then(nc.vector.tensor_tensor(kr[1], kr[1], rot["k2c"], ALU.mult))
                nc.vector.tensor_tensor(kr[0], kr[0], ks[1], ALU.subtract)
                dve_then(nc.vector.tensor_tensor(kr[1], kr[1], ks[0], ALU.add))
                split_block(first["b_in"] + 4)
                up = first["b_up"]

                def key_sums(t):
                    vector.wait_ge(k_squares, t + 1)
                    of = ss_k[:, t * BH:(t + 1) * BH]
                    dve_then(nc.vector.tensor_reduce(of, kc[:, t, :, 0:HD], AX.X, ALU.add))
                    nc.vector.tensor_scalar(of, of, ss_c[:, 4 + t:5 + t], None, ALU.add).then_inc(k_sums, 1)

                def whole_keys(t, h0, h1):
                    vector.wait_ge(qk_rstd, t + 1)
                    if t == 0:
                        vector.wait_ge(up_scalar, 1)
                    else:
                        vector.wait_ge(up_vector, 1)
                    rs = rs_k[:, t * BH + h0:t * BH + h1].unsqueeze(2)
                    nc.vector.tensor_tensor(kc[:, t, h0:h1, 0:HD], kvb[:, t, :].rearrange("p (h c) -> p h c", h=BH)[:, h0:h1, 0:HD],
                                            rs.to_broadcast([P, h1 - h0, HD]), ALU.mult)
                    nc.vector.tensor_tensor(kc[:, t, h0:h1, HD:QK], cb[:, t, 384:416].unsqueeze(1).to_broadcast([P, h1 - h0, 32]),
                                            rs.to_broadcast([P, h1 - h0, 32]), ALU.mult).then_inc(kc_ready, 1)

                def query_sums(t, h0, h1):
                    return nc.vector.tensor_reduce(ss_q[:, q_at(t, h0):q_at(t, h0) + h1 - h0],
                                                   q_sq[t][:, h0 * QK:h1 * QK].rearrange("p (h d) -> p h d", d=QK), AX.X, ALU.add)

                key_sums(0)
                split_latent(2, slice(0, 2), ps[:, 0, :])
                vector.wait_ge(block_used, up + 1)
                nc.vector.tensor_copy(kvb[:, 1, :], ps[:, 4:8, :].rearrange("p b c -> p (b c)")).then_inc(up_vector, 1)
                key_sums(1)
                whole_keys(0, 0, EARLY_KEYS)
                vector.wait_ge(q_squares, 1)
                query_sums(0, 0, EARLY)
                whole_keys(1, 0, EARLY_KEYS)
                vector.wait_ge(up_scalar, 3)
                vector.wait_ge(q_squares, 2)
                n = EARLY * 16
                rope_queries(nc.vector, dve_then, (1,), 0, EARLY,
                             [flat_act[:, 1024 + a:1024 + a + n].rearrange("p (h c) -> p h c", c=16) for a in (0, n)], q_roped)
                query_sums(1, 0, EARLY).then_inc(q_sums, 1)
                vector.wait_ge(q_squares, 4)
                for t in range(TT):
                    last = query_sums(t, EARLY, BH)
                last.then_inc(q_sums, 1)

                def between_vector(n):
                    if n < TT:
                        whole_keys(n, EARLY_KEYS, BH)
                    if 2 <= n < 2 + 3 * QUARTERS:
                        split_quarter(up + 3 + (n - 2) // QUARTERS, (n - 2) % QUARTERS)

                attention_vector(heads_b, between_vector)
                for b in range(first["b_out"], first["b_out"] + 2):
                    split_block(b + 3)
                add_scaled(6, 1.0)
            if "F4" in STAGES:
                ffn_vector("F4", 8, 7, first["b_out"] + 6)

        @block.tensor
        def _(tensor):
            tensor.wait_ge(tables_ready, 1)
            tensor.wait_ge(gain_landed, 16 * len(gain_sources))
            nc.tensor.transpose(ps[:, 7, 0:GAIN_ROWS], gain_rows[:, :], ident[0:GAIN_ROWS, 0:GAIN_ROWS]).then_inc(gain_psum, 1)
            norm_tensor_turn(0, mem)

            def project(p):
                if p >= 4:
                    tensor.wait_ge(proj_out, p - 3)
                b = first["kv"] + p
                wait_h = {0: 0, 2: 4}.get(p)
                if p in PROJ_FEATURES:
                    features_out(b, lambda f: ps[:, 4 + p % 4, f * TOK:(f + 1) * TOK], wait_h=wait_h)
                else:
                    tokens_out(b, lambda t, c, w: ps[:, 4 + p % 4, t * TOK + c:t * TOK + c + w], wait_h=wait_h)

            project(0)
            tensor.wait_ge(h_hi_ready, 4)
            tensor.wait_ge(h_lo_ready, 4)
            norm_tensor_turn(1, x)
            project(1)
            for p in range(2, 11):
                project(p)
                if p == 2:
                    tensor.wait_ge(table_ready, 1)
                if p < 2 + CHUNKS:
                    bias_tensor(p - 2)
            tensor.wait_ge(ws_ready, 1)
            tensor.wait_ge(proj_out, 10)
            for g in range(G):
                nc.tensor.transpose(ps[:, 7 - g // 4 * 2, g % 4 * P:(g % 4 + 1) * P], ws[:, g, :], ident[:, :])
            nc.tensor.transpose(ps[:, 5, 256:262], bs, ident[0:6, 0:6]).then_inc(ws_psum, 1)
            tensor.wait_ge(lf_ready, 1)
            nc.tensor.matmul(ps[0:6, 4, 0:TOK], lf[:, 0, :], tri[:, P:3 * P], start=True, stop=False, skip_group_check=True)
            nc.tensor.matmul(ps[0:6, 4, 0:TOK], lf[:, 1, :], tri[:, 0:2 * P], start=False, stop=True, skip_group_check=True).then_inc(ct_psum, 1)
            tensor.wait_ge(bias_out, CHUNKS - 1)
            tensor.wait_ge(proj_out, 11)

            def gated_turn(n):
                if n == 1:
                    tensor.wait_ge(v_ready, 1)
                    tensor.wait_ge(ws_t_ready, 3)
                    for t in range(TT):
                        for g in range(G):
                            last = nc.tensor.matmul(ps[:, 6 + t, g * HD:(g + 1) * HD], ws_t[:, g, :], uv[:, t, 384 + g * HD:384 + (g + 1) * HD],
                                                    start=True, stop=True, skip_group_check=True)
                    last.then_inc(mixed_psum, 1)
                    tensor.wait_ge(nct_ready, 1)
                    tensor.wait_ge(bias_out, CHUNKS)
                    tensor.wait_ge(tables_ready, 2)
                if n == 4:
                    tensor.wait_ge(oa_ready, 1)
                    for k in range(3):
                        for t in range(TT):
                            last = nc.tensor.transpose(ps[:, 6 + k // 2, k % 2 * TOK + t * P:k % 2 * TOK + (t + 1) * P],
                                                       oa[:, t, k * P:(k + 1) * P], ident[:, :])
                    last.then_inc(oa_psum, 1)

            attention_tensor(heads_m1, gated_turn)

            def output_projection(stage, wait_k):
                for c in range(4):
                    tokens_out(first[stage] + c, lambda t, c0, w: y_bank(t, 256 * c + c0, w),
                               wait_k=wait_k if c == 0 else None, half_done=y_tile if c == 3 else None)

            def wait_m1(k):
                if k == 0:
                    tensor.wait_ge(oa_lo, 2)
                if 3 <= k < 6:
                    tensor.wait_ge(o_lo_ready, k)

            output_projection("out", wait_m1)
            if "F0" in STAGES:
                norm_tensor_turn(2, x)
                relu_steps(tensor, relu_tensor)
                second_product("F0", b_down(I0 - 1), I0 - 1, (I0 - 1) % 3, False, True)

            def ffn_tensor(st, n):
                norm_tensor_turn(n, x)
                swiglu_steps(tensor, st, lambda st, s, turn=0: swiglu_tensor(st, n, s, turn))
                second_product(st, b_lower(st, I1 - 1), I1 - 1, (I1 - 1) % 2, False, True)

            if "F1" in STAGES:
                ffn_tensor("F1", 3)
            if "MA" in STAGES:
                norm_tensor_turn(4, x)

                def turn_a(p):
                    tensor.wait_ge(a_scaled, p + 1)
                    if p >= 3:
                        tensor.wait_ge(a_squares, p)
                    for k in range(2):
                        for t in range(TT):
                            c = k * P
                            source = qa[:, t, 256 * (p - 1) + c:256 * (p - 1) + c + P] if p else kd[:, t, c:c + P]
                            last = nc.tensor.transpose(ps[:, A_TURN_BANK[p], k * TOK + t * P:k * TOK + (t + 1) * P], source, ident[:, :])
                    last.then_inc(a_turned, 1)

                for p in range(5):
                    if p >= 4:
                        tensor.wait_ge(a_squares, p - 3)
                    tokens_out(first["a_in"] + p, lambda t, c, w: ps[:, 4 + p % 4, t * TOK + c:t * TOK + c + w],
                               wait_h=16 if p == 0 else None)
                    if p >= 2:
                        turn_a(p - 2)

                def late_turns(n):
                    if n < 2:
                        turn_a(n + 3)
                    if n == 1:
                        tensor.wait_ge(a_turned_out, 3)

                attention_tensor(heads_a, late_turns)
                output_projection("a_out", lambda k: tensor.wait_ge(o_lo_ready, 5 + k + 1))
            if "F2" in STAGES:
                ffn_tensor("F2", 5)
                ffn_tensor("F3", 6)
            if "MB" in STAGES:
                norm_tensor_turn(7, x)
                for p in range(2):
                    tokens_out(first["b_in"] + p, lambda t, c, w: ps[:, 4 + p, t * TOK + c:t * TOK + c + w],
                               wait_h=28 if p == 0 else None)

                def turn_latent(n, chunks, bank):
                    tensor.wait_ge(cn_ready, n)
                    for k in chunks:
                        for t in range(TT):
                            col = (k - chunks[0]) * TOK + t * P
                            last = nc.tensor.transpose(ps[:, bank, col:col + P], cn[:, t, k * P:(k + 1) * P], ident[:, :])
                    last.then_inc(c_turned, 1)
                    tensor.wait_ge(c_lo, n)

                up = first["b_up"]
                turn_latent(1, [2], 7)
                tokens_out(up, lambda t, c, w: ps[:, 4 * t + c // 512, 0:w], h0=2, half_done=up_half,
                           before=lambda: tensor.wait_ge(c_squares, 6))
                tensor.wait_ge(k_squares, 1)
                turn_latent(2, [0, 1], 0)
                tokens_out(up + 1, lambda t, c, w: ps[:, 2 + 2 * t + c // 512, 0:w], half_done=up_half,
                           before=lambda: tensor.wait_ge(up_vector, 1))
                tokens_out(up + 2, lambda t, c, w: ps[:, t, 0:w])
                tensor.wait_ge(q_squares, 4)
                tensor.wait_ge(kc_ready, 2)
                tensor.wait_ge(q_roped_first, 1)
                tensor.wait_ge(q_roped, 1)
                turn_qk_tensor(0)
                turn_qk_tensor(1)
                attention_tensor(heads_b, lambda n: turn_qk_tensor(n + 2))
                output_projection("b_out", lambda k: tensor.wait_ge(o_lo_ready, 13 + k + 1))
            if "F4" in STAGES:
                ffn_tensor("F4", 8)


def kernel(**inputs):
    import numpy as np
    import concourse.bacc as bacc
    from concourse.bass_utils import run_bass_kernel_spmd

    nc = bacc.Bacc("TRN2", target_bir_lowering=False, num_devices=1)
    arrays, args = {}, {}
    for name, value in inputs.items():
        a = np.ascontiguousarray(value)
        arrays[f"in_{name}"] = a
        args[name] = nc.dram_tensor(f"in_{name}", a.shape, mybir.dt.from_np(a.dtype), kind="ExternalInput").ap()
    first_of = [-3.0e38] + [float(k if k <= 16 else math.ceil(16 * 8 ** ((k - 16) / 16))) for k in range(1, 32)]
    pairs = np.array([[a, b] for a, b in zip(first_of, first_of[1:] + [3.0e38])], np.float32)
    constants = {"bucket_edges": np.concatenate([pairs] * 4),
                 "rope_freq": (np.float32(10000.0) ** (-np.arange(0, 32, 2, dtype=np.float32) / np.float32(32)))[None, :]}
    for name, a in constants.items():
        arrays[f"const_{name}"] = a
        args[name] = nc.dram_tensor(f"const_{name}", a.shape, F32, kind="ExternalInput").ap()
    out = nc.dram_tensor("out", (TOK, D), F32, kind="ExternalOutput").ap()
    build(nc, args, out)
    r = run_bass_kernel_spmd(nc, [arrays], core_ids=[0])
    return r.results[0]["out"].reshape(1, TOK, D)
```
